# Optimizing a Trainium2 kernel written in Bass

```python
import jax, jax.numpy as jnp
from jax import lax
import numpy as np
import math

D_MODEL = 1024
BATCH = 1
SEQ = 256
DEPTH = 2

N_GROUPS = 4
GROUP_HEADS = 4
GROUP_WIDTH = D_MODEL // N_GROUPS
HEAD_DIM = GROUP_WIDTH // GROUP_HEADS
MIX_WIDTH = N_GROUPS * GROUP_WIDTH
CONV_WIDTH = 3
RWKV_DECAY_RANK = 64
RWKV_ICLR_RANK = 64
RWKV_GATE_RANK = 128
RWKV_GN_EPS = 64e-5
RET_CHUNK = 128
MLA_Q_RANK = 384
MLA_KV_RANK = 128
MLA_NOPE = 64
MLA_ROPE = 32
MLA_V = 64
ATTN_BLOCK = 128
D_FF = 2816
ROPE_BASE = 10000.0
NORM_EPS = 1e-6
MAX_POS_OFFSET = 4096
IN_SPLITS = (
    GROUP_WIDTH, GROUP_WIDTH, GROUP_WIDTH,
    GROUP_WIDTH, GROUP_WIDTH, GROUP_WIDTH,
    RWKV_DECAY_RANK, RWKV_DECAY_RANK,
    RWKV_ICLR_RANK, RWKV_ICLR_RANK,
    RWKV_GATE_RANK,
    GROUP_WIDTH, GROUP_WIDTH, GROUP_WIDTH, GROUP_WIDTH,
    MLA_Q_RANK, MLA_KV_RANK + MLA_ROPE,
)
IN_WIDTH = sum(IN_SPLITS)


def rmsnorm(x, g):
    xf = x.astype(jnp.float32)
    y = xf * lax.rsqrt(jnp.mean(xf * xf, axis=-1, keepdims=True) + NORM_EPS)
    return (y * g.astype(jnp.float32)).astype(x.dtype)

def swiglu(x, w_gate, w_up, w_down):
    return (jax.nn.silu(x @ w_gate) * (x @ w_up)) @ w_down

def rope(x, pos):
    half = x.shape[-1] // 2
    inv = ROPE_BASE ** (-jnp.arange(half, dtype=jnp.float32) / half)
    ang = pos.astype(jnp.float32)[:, :, None, None] * inv
    cos, sin = jnp.cos(ang), jnp.sin(ang)
    xf = x.astype(jnp.float32)
    x1, x2 = xf[..., :half], xf[..., half:]
    return jnp.concatenate([x1 * cos - x2 * sin, x1 * sin + x2 * cos], axis=-1).astype(x.dtype)

def heads(t):
    b, s, _ = t.shape
    return t.reshape(b, s, GROUP_HEADS, HEAD_DIM).astype(jnp.float32)

def short_conv_mixer(x_in, b_gate, c_gate, conv_w):
    u = c_gate * x_in
    y = lax.conv_general_dilated(
        u, conv_w[:, None, :].astype(u.dtype), window_strides=(1,), padding=[(1, 1)],
        dimension_numbers=('NWC', 'WIO', 'NWC'), feature_group_count=GROUP_WIDTH)
    return b_gate * y

def rwkv7_scan(r, k, v, kk, a, decay, reverse):
    xs = tuple(jnp.moveaxis(t, 1, 0) for t in (r, k, v, kk, a, decay))
    b, _, h, n = r.shape

    def step(S, inp):
        r_t, k_t, v_t, kk_t, a_t, w_t = inp
        sa = jnp.einsum('bhvk,bhk->bhv', S, -kk_t)
        S = (S * w_t[:, :, None, :] + sa[..., None] * (kk_t * a_t)[:, :, None, :]
             + v_t[..., None] * k_t[:, :, None, :])
        return S, jnp.einsum('bhvk,bhk->bhv', S, r_t)

    S0 = jnp.zeros((b, h, n, n), jnp.float32)
    _, y = lax.scan(step, S0, xs, reverse=reverse)
    return jnp.moveaxis(y, 0, 1)

def rwkv7_mixer(r, k, v, wd_f, wd_b, ad_f, ad_b, gd, w0_f, w0_b, w2_f, w2_b,
                a0_f, a0_b, a2_f, a2_b, g2, k_k, k_a, r_k, lnx_g, lnx_b):
    b, s, _ = r.shape
    g = jax.nn.sigmoid(gd) @ g2
    kk = heads(k * k_k)
    kk = kk / jnp.maximum(jnp.sqrt(jnp.sum(kk * kk, axis=-1, keepdims=True)), 1e-12)
    rh, vh = heads(r), heads(v)
    y = jnp.zeros_like(rh)
    k_sum = jnp.zeros_like(rh)
    for wd, ad, w0, w2, a0, a2, rev in ((wd_f, ad_f, w0_f, w2_f, a0_f, a2_f, False),
                                        (wd_b, ad_b, w0_b, w2_b, a0_b, a2_b, True)):
        w_log = -jax.nn.softplus(-(w0 + jnp.tanh(wd) @ w2)) - 0.5
        decay = jnp.exp(-jnp.exp(w_log.astype(jnp.float32)))
        a = jax.nn.sigmoid(a0 + ad @ a2)
        k_dir = heads(k * (1.0 + (a - 1.0) * k_a))
        y = y + rwkv7_scan(rh, k_dir, vh, kk, heads(a), heads(decay), rev)
        k_sum = k_sum + k_dir
    mu = jnp.mean(y, axis=-1, keepdims=True)
    var = jnp.mean(jnp.square(y - mu), axis=-1, keepdims=True)
    yn = ((y - mu) * lax.rsqrt(var + RWKV_GN_EPS)).reshape(b, s, GROUP_WIDTH)
    yn = yn * lnx_g.astype(jnp.float32) + lnx_b.astype(jnp.float32)
    bonus = (jnp.sum(rh * k_sum * r_k.astype(jnp.float32), axis=-1, keepdims=True) * vh).reshape(b, s, GROUP_WIDTH)
    return (yn + bonus).astype(r.dtype) * g

def retention_mixer(q, k, v, g, pos, gn_g):
    b, s, _ = q.shape
    nc, C = s // RET_CHUNK, RET_CHUNK
    qh = rope(q.reshape(b, s, GROUP_HEADS, HEAD_DIM), pos)
    kh = rope(k.reshape(b, s, GROUP_HEADS, HEAD_DIM), pos) * (HEAD_DIM ** -0.5)
    vh = v.reshape(b, s, GROUP_HEADS, HEAD_DIM)
    chunk = lambda t: t.reshape(b, nc, C, GROUP_HEADS, HEAD_DIM).transpose(0, 3, 1, 2, 4).astype(jnp.float32)
    qc, kc, vc = chunk(qh), chunk(kh), chunk(vh)
    log_gamma = jnp.log(1.0 - 2.0 ** (-5.0 - jnp.arange(GROUP_HEADS, dtype=jnp.float32)))
    idx = jnp.arange(C, dtype=jnp.float32)
    intra_decay = jnp.exp(log_gamma[:, None, None] * jnp.abs(idx[:, None] - idx[None, :]))
    dec_start = jnp.exp(log_gamma[:, None] * idx)[None, :, None, :, None]
    dec_end = jnp.exp(log_gamma[:, None] * (C - idx))[None, :, None, :, None]
    chunk_decay = jnp.exp(log_gamma * C)[None, :, None, None]
    scores = jnp.einsum('bhnid,bhnjd->bhnij', qc, kc) * intra_decay[None, :, None]
    o = jnp.einsum('bhnij,bhnjd->bhnid', scores, vc)
    kv_f = jnp.einsum('bhnjd,bhnje->nbhde', kc * dec_end, vc)
    kv_b = jnp.einsum('bhnjd,bhnje->nbhde', kc * dec_start, vc)

    def step(R, summ):
        return R * chunk_decay + summ, R

    R0 = jnp.zeros((b, GROUP_HEADS, HEAD_DIM, HEAD_DIM), jnp.float32)
    _, R_f = lax.scan(step, R0, kv_f)
    _, R_b = lax.scan(step, R0, kv_b, reverse=True)
    o = (o + dec_start * jnp.einsum('bhnid,nbhde->bhnie', qc, R_f)
         + dec_end * jnp.einsum('bhnid,nbhde->bhnie', qc, R_b))
    o = o.transpose(0, 2, 3, 1, 4).reshape(b, s, GROUP_HEADS, HEAD_DIM)
    o = o * lax.rsqrt(jnp.mean(o * o, axis=-1, keepdims=True) + NORM_EPS)
    o = o.reshape(b, s, GROUP_WIDTH) * gn_g.astype(jnp.float32)
    return jax.nn.silu(g) * o.astype(q.dtype)

def mla_mixer(q_a, kv_a, pos, q_a_norm, q_b, kv_a_norm, kv_b):
    b, s, _ = q_a.shape
    q = (rmsnorm(q_a, q_a_norm) @ q_b).reshape(b, s, GROUP_HEADS, MLA_NOPE + MLA_ROPE)
    q_nope, q_rope = q[..., :MLA_NOPE], rope(q[..., MLA_NOPE:], pos)
    c_kv, k_rope = kv_a[..., :MLA_KV_RANK], kv_a[..., MLA_KV_RANK:]
    kv = (rmsnorm(c_kv, kv_a_norm) @ kv_b).reshape(b, s, GROUP_HEADS, MLA_NOPE + MLA_V)
    k_nope, v = kv[..., :MLA_NOPE], kv[..., MLA_NOPE:]
    k_rope = rope(k_rope[:, :, None, :], pos)[:, :, 0]
    scale = (MLA_NOPE + MLA_ROPE) ** -0.5
    nb = s // ATTN_BLOCK
    blocks = lambda t: t.reshape(b, nb, ATTN_BLOCK, GROUP_HEADS, t.shape[-1]).transpose(1, 0, 2, 3, 4)

    def attend(blk):
        qn, qr = blk
        sc = jnp.einsum('bqhd,bkhd->bhqk', qn, k_nope) + jnp.einsum('bqhr,bkr->bhqk', qr, k_rope)
        p = jax.nn.softmax(sc.astype(jnp.float32) * scale, axis=-1)
        return jnp.einsum('bhqk,bkhd->bqhd', p.astype(v.dtype), v)

    o = lax.map(attend, (blocks(q_nope), blocks(q_rope)))
    return o.transpose(1, 0, 2, 3, 4).reshape(b, s, GROUP_WIDTH)

def first_inputs(seed: int = 0) -> dict:
    key = jax.random.key(seed)
    ks = iter(jax.random.split(key, 48))
    L, W, H, N = DEPTH, GROUP_WIDTH, GROUP_HEADS, HEAD_DIM
    f32 = jnp.float32

    def nrm(shape):
        return jax.random.normal(next(ks), shape, f32)

    def dense(shape, fan_in, scale=1.0):
        return nrm(shape) * (scale * fan_in ** -0.5)

    def gain(shape):
        return 1.0 + 0.02 * nrm(shape)

    decay_base = jnp.tile(jnp.linspace(-6.0, -1.0, N, dtype=f32), H)
    x = nrm((BATCH, SEQ, D_MODEL))
    offsets = jax.random.randint(next(ks), (BATCH, 1), 0, MAX_POS_OFFSET, dtype=jnp.int32)
    positions = offsets + jnp.arange(SEQ, dtype=jnp.int32)[None, :]
    return {
        'x': x,
        'positions': positions,
        'ffn1_norm': gain((L, D_MODEL)),
        'ffn1_w_gate': dense((L, D_MODEL, D_FF), D_MODEL),
        'ffn1_w_up': dense((L, D_MODEL, D_FF), D_MODEL),
        'ffn1_w_down': dense((L, D_FF, D_MODEL), D_FF),
        'mix_norm': gain((L, D_MODEL)),
        'w_in': dense((L, D_MODEL, IN_WIDTH), D_MODEL),
        'w_out': dense((L, MIX_WIDTH, D_MODEL), MIX_WIDTH),
        'conv_w': dense((L, CONV_WIDTH, W), CONV_WIDTH),
        'rwkv_w0_f': decay_base + 0.1 * nrm((L, W)),
        'rwkv_w0_b': decay_base + 0.1 * nrm((L, W)),
        'rwkv_w2_f': dense((L, RWKV_DECAY_RANK, W), RWKV_DECAY_RANK, 0.1),
        'rwkv_w2_b': dense((L, RWKV_DECAY_RANK, W), RWKV_DECAY_RANK, 0.1),
        'rwkv_a0_f': 0.1 * nrm((L, W)),
        'rwkv_a0_b': 0.1 * nrm((L, W)),
        'rwkv_a2_f': dense((L, RWKV_ICLR_RANK, W), RWKV_ICLR_RANK, 0.1),
        'rwkv_a2_b': dense((L, RWKV_ICLR_RANK, W), RWKV_ICLR_RANK, 0.1),
        'rwkv_g2': dense((L, RWKV_GATE_RANK, W), RWKV_GATE_RANK),
        'rwkv_k_k': 0.85 + 0.02 * nrm((L, W)),
        'rwkv_k_a': 1.0 + 0.02 * nrm((L, W)),
        'rwkv_r_k': 0.1 * nrm((L, H, N)),
        'rwkv_lnx_g': gain((L, W)),
        'rwkv_lnx_b': 0.01 * nrm((L, W)),
        'ret_gn_g': gain((L, W)),
        'mla_q_a_norm': gain((L, MLA_Q_RANK)),
        'mla_q_b': dense((L, MLA_Q_RANK, H * (MLA_NOPE + MLA_ROPE)), MLA_Q_RANK),
        'mla_kv_a_norm': gain((L, MLA_KV_RANK)),
        'mla_kv_b': dense((L, MLA_KV_RANK, H * (MLA_NOPE + MLA_V)), MLA_KV_RANK),
        'ffn2_norm': gain((L, D_MODEL)),
        'ffn2_w_gate': dense((L, D_MODEL, D_FF), D_MODEL),
        'ffn2_w_up': dense((L, D_MODEL, D_FF), D_MODEL),
        'ffn2_w_down': dense((L, D_FF, D_MODEL), D_FF),
        'final_norm': gain((D_MODEL,)),
    }

def first_block(x, positions, ffn1_norm, ffn1_w_gate, ffn1_w_up, ffn1_w_down, mix_norm, w_in, w_out,
              conv_w, rwkv_w0_f, rwkv_w0_b, rwkv_w2_f, rwkv_w2_b, rwkv_a0_f, rwkv_a0_b, rwkv_a2_f,
              rwkv_a2_b, rwkv_g2, rwkv_k_k, rwkv_k_a, rwkv_r_k, rwkv_lnx_g, rwkv_lnx_b, ret_gn_g,
              mla_q_a_norm, mla_q_b, mla_kv_a_norm, mla_kv_b, ffn2_norm, ffn2_w_gate, ffn2_w_up,
              ffn2_w_down, final_norm):
    split_points = tuple(int(p) for p in np.cumsum(IN_SPLITS)[:-1])
    for l in range(DEPTH):
        x = x + 0.5 * swiglu(rmsnorm(x, ffn1_norm[l]), ffn1_w_gate[l], ffn1_w_up[l], ffn1_w_down[l])
        h = rmsnorm(x, mix_norm[l])
        u = h @ w_in[l]
        (c_x, c_b, c_c, rw_r, rw_k, rw_v, rw_wd_f, rw_wd_b, rw_ad_f, rw_ad_b, rw_gd,
         rt_q, rt_k, rt_v, rt_g, ml_qa, ml_kva) = jnp.split(u, split_points, axis=-1)
        y_conv = short_conv_mixer(c_x, c_b, c_c, conv_w[l])
        y_rwkv = rwkv7_mixer(rw_r, rw_k, rw_v, rw_wd_f, rw_wd_b, rw_ad_f, rw_ad_b, rw_gd,
                             rwkv_w0_f[l], rwkv_w0_b[l], rwkv_w2_f[l], rwkv_w2_b[l],
                             rwkv_a0_f[l], rwkv_a0_b[l], rwkv_a2_f[l], rwkv_a2_b[l], rwkv_g2[l],
                             rwkv_k_k[l], rwkv_k_a[l], rwkv_r_k[l], rwkv_lnx_g[l], rwkv_lnx_b[l])
        y_ret = retention_mixer(rt_q, rt_k, rt_v, rt_g, positions, ret_gn_g[l])
        y_mla = mla_mixer(ml_qa, ml_kva, positions, mla_q_a_norm[l], mla_q_b[l], mla_kv_a_norm[l], mla_kv_b[l])
        x = x + jnp.concatenate([y_conv, y_rwkv, y_ret, y_mla], axis=-1) @ w_out[l]
        x = x + 0.5 * swiglu(rmsnorm(x, ffn2_norm[l]), ffn2_w_gate[l], ffn2_w_up[l], ffn2_w_down[l])
    return rmsnorm(x, final_norm)


N_MIXERS = 2
N_POOL_LAYERS = (DEPTH + 1) // 2
N_DN_LAYERS = DEPTH // 2

RMS_EPS = 1e-6

POOL_WINDOWS = (2, 4, 8, 16)
POOL_GROUPS = len(POOL_WINDOWS)
POOL_GROUP_DIM = D_MODEL // POOL_GROUPS

DN_HEAD_DIM = 128
DN_HEADS = D_MODEL // DN_HEAD_DIM
DN_KEY_DIM = DN_HEADS * DN_HEAD_DIM
DN_CONV = 4
DN_CHUNK = 64
DN_IN_DIM = 4 * DN_KEY_DIM + 2 * DN_HEADS

DENSE_FF = 2816
N_EXPERTS = 8
TOP_K = 2
EXPERT_FF = 3584


def rmsnorm_2(x, g):
    x32 = x.astype(jnp.float32)
    y = x32 * lax.rsqrt(jnp.mean(x32 * x32, axis=-1, keepdims=True) + RMS_EPS)
    return (y * g.astype(jnp.float32)).astype(x.dtype)

def l2norm(x):
    return x * lax.rsqrt(jnp.sum(x * x, axis=-1, keepdims=True) + RMS_EPS)

def swiglu_2(x, w_gate, w_up, w_down):
    return (jax.nn.silu(x @ w_gate) * (x @ w_up)) @ w_down

def pool_mixer(h, w_in, w_group, scale):
    b, s, d = h.shape
    u = (h @ w_in).reshape(b, s, POOL_GROUPS, POOL_GROUP_DIM).astype(jnp.float32)
    csum = jnp.cumsum(u, axis=1)
    pos = jnp.arange(1, s + 1, dtype=jnp.float32)[:, None]
    outs = []
    for gi, w in enumerate(POOL_WINDOWS):
        c = csum[:, :, gi]
        c_prev = jnp.pad(c, ((0, 0), (w, 0), (0, 0)))[:, :s]
        cnt = jnp.minimum(pos, float(w))
        outs.append((c - c_prev) / cnt - u[:, :, gi])
    m = jnp.stack(outs, axis=2).astype(h.dtype)
    y = jnp.einsum('bsgc,gce->bsge', m, w_group).reshape(b, s, d)
    return y * scale

def causal_depthwise_conv(x, w):
    k, c = w.shape
    return lax.conv_general_dilated(
        x, w[:, None, :], window_strides=(1,), padding=[(k - 1, 0)],
        dimension_numbers=('NWC', 'WIO', 'NWC'), feature_group_count=c)

def gated_delta_rule_chunked(q, k, v, beta, g):
    b, s, h, dk = q.shape
    dv = v.shape[-1]
    c = DN_CHUNK
    n = s // c

    def to_chunks(t):
        t = t.reshape((b, n, c, h) + t.shape[3:])
        return jnp.moveaxis(t, 3, 1)

    q, k, v, beta, g = (to_chunks(t) for t in (q, k, v, beta, g))
    gc = jnp.cumsum(g, axis=-1)
    causal = jnp.tril(jnp.ones((c, c), dtype=bool))
    strict = jnp.tril(jnp.ones((c, c), dtype=bool), -1)
    decay = jnp.exp(jnp.where(causal, gc[..., :, None] - gc[..., None, :], -jnp.inf))

    k_beta = k * beta[..., None]
    v_beta = v * beta[..., None]
    a = jnp.einsum('bhnid,bhnjd->bhnij', k_beta, k) * decay
    a = jnp.where(strict, a, 0.0) + jnp.eye(c, dtype=a.dtype)
    u = lax.linalg.triangular_solve(a, v_beta, left_side=True, lower=True, unit_diagonal=True)
    w = lax.linalg.triangular_solve(a, k_beta * jnp.exp(gc)[..., None],
                                    left_side=True, lower=True, unit_diagonal=True)
    qk = jnp.einsum('bhnid,bhnjd->bhnij', q, k) * decay

    xs = tuple(jnp.moveaxis(t, 2, 0) for t in (q, k, u, w, qk, gc))

    def step(state, inp):
        q_c, k_c, u_c, w_c, qk_c, gc_c = inp
        v_new = u_c - jnp.einsum('bhck,bhkv->bhcv', w_c, state)
        o = (jnp.einsum('bhck,bhkv->bhcv', q_c * jnp.exp(gc_c)[..., None], state)
             + jnp.einsum('bhij,bhjv->bhiv', qk_c, v_new))
        g_last = gc_c[..., -1]
        k_dec = k_c * jnp.exp(g_last[..., None] - gc_c)[..., None]
        state = state * jnp.exp(g_last)[..., None, None] + jnp.einsum('bhck,bhcv->bhkv', k_dec, v_new)
        return state, o

    s0 = jnp.zeros((b, h, dk, dv), jnp.float32)
    _, o = lax.scan(step, s0, xs)
    return jnp.transpose(o, (1, 0, 3, 2, 4)).reshape(b, s, h, dv)

def deltanet_mixer(h, w_in, conv_w, a_log, dt_bias, norm_g, w_out):
    b, s, _ = h.shape
    kd = DN_KEY_DIM
    proj = h @ w_in
    qkv = proj[..., :3 * kd]
    z = proj[..., 3 * kd:4 * kd]
    b_logit = proj[..., 4 * kd:4 * kd + DN_HEADS].astype(jnp.float32)
    a_in = proj[..., 4 * kd + DN_HEADS:].astype(jnp.float32)
    qkv = jax.nn.silu(causal_depthwise_conv(qkv, conv_w)).astype(jnp.float32)
    q, k, v = jnp.split(qkv, 3, axis=-1)
    q = l2norm(q.reshape(b, s, DN_HEADS, DN_HEAD_DIM)) * (DN_HEAD_DIM ** -0.5)
    k = l2norm(k.reshape(b, s, DN_HEADS, DN_HEAD_DIM))
    v = v.reshape(b, s, DN_HEADS, DN_HEAD_DIM)
    beta = jax.nn.sigmoid(b_logit)
    g = -jnp.exp(a_log.astype(jnp.float32)) * jax.nn.softplus(a_in + dt_bias.astype(jnp.float32))
    o = gated_delta_rule_chunked(q, k, v, beta, g)
    o = o * lax.rsqrt(jnp.mean(o * o, axis=-1, keepdims=True) + RMS_EPS) * norm_g.astype(jnp.float32)
    o = o * jax.nn.silu(z.astype(jnp.float32)).reshape(b, s, DN_HEADS, DN_HEAD_DIM)
    return o.reshape(b, s, kd).astype(h.dtype) @ w_out

def moe_ffn(h, router_w, router_b, w_gate, w_up, w_down):
    b, s, d = h.shape
    t = h.reshape(b * s, d)
    logits = (t @ router_w).astype(jnp.float32) + router_b.astype(jnp.float32)
    top_vals, top_idx = lax.top_k(logits, TOP_K)
    top_w = jax.nn.softmax(top_vals, axis=-1)
    gates = jnp.sum(jax.nn.one_hot(top_idx, N_EXPERTS, dtype=jnp.float32) * top_w[..., None], axis=1)
    out = jnp.zeros((b * s, d), jnp.float32)
    for e in range(N_EXPERTS):
        y = swiglu_2(t, w_gate[e], w_up[e], w_down[e]).astype(jnp.float32)
        out = out + gates[:, e:e + 1] * y
    return out.astype(h.dtype).reshape(b, s, d)

def second_inputs(seed: int = 0) -> dict:
    key = jax.random.key(seed)
    ks = jax.random.split(key, 24)
    f32 = jnp.float32
    D = D_MODEL
    NP, ND = N_POOL_LAYERS, N_DN_LAYERS

    def nrm(k, shape, fan_in):
        return jax.random.normal(k, shape, f32) * (fan_in ** -0.5)

    def gain(k, shape):
        return 1.0 + 0.05 * jax.random.normal(k, shape, f32)

    dt = jnp.exp(jax.random.uniform(ks[10], (ND, DN_HEADS), f32,
                                    minval=math.log(1e-3), maxval=math.log(1e-1)))
    return {
        "x": jax.random.normal(ks[0], (BATCH, SEQ, D), f32),
        "norm_mix_g": gain(ks[1], (DEPTH, D)),
        "norm_ffn_g": gain(ks[2], (DEPTH, D)),
        "pool_w_in": nrm(ks[3], (NP, D, D), D),
        "pool_w_group": nrm(ks[4], (NP, POOL_GROUPS, POOL_GROUP_DIM, POOL_GROUP_DIM), POOL_GROUP_DIM),
        "pool_scale": gain(ks[5], (NP, D)),
        "dn_w_in": nrm(ks[6], (ND, D, DN_IN_DIM), D),
        "dn_conv_w": nrm(ks[7], (ND, DN_CONV, 3 * DN_KEY_DIM), DN_CONV),
        "dn_a_log": jnp.log(jax.random.uniform(ks[8], (ND, DN_HEADS), f32, minval=1.0, maxval=16.0)),
        "dn_dt_bias": dt + jnp.log(-jnp.expm1(-dt)),
        "dn_norm_g": gain(ks[9], (ND, DN_HEAD_DIM)),
        "dn_w_out": nrm(ks[11], (ND, DN_KEY_DIM, D), DN_KEY_DIM),
        "ffn_w_gate": nrm(ks[12], (NP, D, DENSE_FF), D),
        "ffn_w_up": nrm(ks[13], (NP, D, DENSE_FF), D),
        "ffn_w_down": nrm(ks[14], (NP, DENSE_FF, D), DENSE_FF),
        "moe_router_w": nrm(ks[15], (ND, D, N_EXPERTS), D),
        "moe_router_b": 0.01 * jax.random.normal(ks[16], (ND, N_EXPERTS), f32),
        "moe_w_gate": nrm(ks[17], (ND, N_EXPERTS, D, EXPERT_FF), D),
        "moe_w_up": nrm(ks[18], (ND, N_EXPERTS, D, EXPERT_FF), D),
        "moe_w_down": nrm(ks[19], (ND, N_EXPERTS, EXPERT_FF, D), EXPERT_FF),
        "final_norm_g": gain(ks[20], (D,)),
    }

def second_block(x, norm_mix_g, norm_ffn_g, pool_w_in, pool_w_group, pool_scale,
              dn_w_in, dn_conv_w, dn_a_log, dn_dt_bias, dn_norm_g, dn_w_out,
              ffn_w_gate, ffn_w_up, ffn_w_down,
              moe_router_w, moe_router_b, moe_w_gate, moe_w_up, moe_w_down,
              final_norm_g):
    h = x
    for i in range(DEPTH):
        j = i // N_MIXERS
        hn = rmsnorm_2(h, norm_mix_g[i])
        if i % N_MIXERS == 0:
            h = h + pool_mixer(hn, pool_w_in[j], pool_w_group[j], pool_scale[j])
        else:
            h = h + deltanet_mixer(hn, dn_w_in[j], dn_conv_w[j], dn_a_log[j], dn_dt_bias[j],
                                   dn_norm_g[j], dn_w_out[j])
        hn = rmsnorm_2(h, norm_ffn_g[i])
        if i % 2 == 0:
            h = h + swiglu_2(hn, ffn_w_gate[j], ffn_w_up[j], ffn_w_down[j])
        else:
            h = h + moe_ffn(hn, moe_router_w[j], moe_router_b[j], moe_w_gate[j], moe_w_up[j], moe_w_down[j])
    return rmsnorm_2(h, final_norm_g)


def setup_inputs(seed=0):
    out = dict(first_inputs(seed))
    for name, value in second_inputs(seed + 1).items():
        if name != "x":
            out[name + "_2"] = value
    return out


def reference(
    x, positions, ffn1_norm, ffn1_w_gate, ffn1_w_up, ffn1_w_down, mix_norm, w_in, w_out, conv_w,
    rwkv_w0_f, rwkv_w0_b, rwkv_w2_f, rwkv_w2_b, rwkv_a0_f, rwkv_a0_b, rwkv_a2_f, rwkv_a2_b,
    rwkv_g2, rwkv_k_k, rwkv_k_a, rwkv_r_k, rwkv_lnx_g, rwkv_lnx_b, ret_gn_g, mla_q_a_norm,
    mla_q_b, mla_kv_a_norm, mla_kv_b, ffn2_norm, ffn2_w_gate, ffn2_w_up, ffn2_w_down,
    final_norm, norm_mix_g_2, norm_ffn_g_2, pool_w_in_2, pool_w_group_2, pool_scale_2,
    dn_w_in_2, dn_conv_w_2, dn_a_log_2, dn_dt_bias_2, dn_norm_g_2, dn_w_out_2, ffn_w_gate_2,
    ffn_w_up_2, ffn_w_down_2, moe_router_w_2, moe_router_b_2, moe_w_gate_2, moe_w_up_2,
    moe_w_down_2, final_norm_g_2,
):
    x = first_block(
        x, positions, ffn1_norm, ffn1_w_gate, ffn1_w_up, ffn1_w_down, mix_norm, w_in, w_out,
        conv_w, rwkv_w0_f, rwkv_w0_b, rwkv_w2_f, rwkv_w2_b, rwkv_a0_f, rwkv_a0_b, rwkv_a2_f,
        rwkv_a2_b, rwkv_g2, rwkv_k_k, rwkv_k_a, rwkv_r_k, rwkv_lnx_g, rwkv_lnx_b, ret_gn_g,
        mla_q_a_norm, mla_q_b, mla_kv_a_norm, mla_kv_b, ffn2_norm, ffn2_w_gate, ffn2_w_up,
        ffn2_w_down, final_norm,
    )
    return second_block(
        x, norm_mix_g_2, norm_ffn_g_2, pool_w_in_2, pool_w_group_2, pool_scale_2, dn_w_in_2,
        dn_conv_w_2, dn_a_log_2, dn_dt_bias_2, dn_norm_g_2, dn_w_out_2, ffn_w_gate_2,
        ffn_w_up_2, ffn_w_down_2, moe_router_w_2, moe_router_b_2, moe_w_gate_2, moe_w_up_2,
        moe_w_down_2, final_norm_g_2,
    )


_drawn_inputs = setup_inputs


def setup_inputs(seed=0):
    import zlib

    import numpy as np

    out = dict(_drawn_inputs(seed))
    spreads = {}
    factors = {'rwkv_w2_f': 22.199,
     'rwkv_w2_b': 8.0,
     'rwkv_a2_b': 2.682,
     'rwkv_k_k': 87.629,
     'rwkv_lnx_b': 5.166,
     'ret_gn_g': 3.316,
     'mla_q_a_norm': 8.0,
     'mla_kv_a_norm': 4.969,
     'moe_router_b_2': 5.485,
     'rwkv_k_a': 2.718,
     'rwkv_lnx_g': 2.687}
    for name, (base, spread) in spreads.items():
        noise = np.random.default_rng([zlib.crc32(name.encode()), seed]).standard_normal(out[name].shape)
        drawn = base * np.exp(spread * noise) if base else spread * noise
        out[name] = __import__('jax').numpy.asarray(drawn.astype(out[name].dtype))
    for name, factor in factors.items():
        out[name] = (out[name] * factor).astype(out[name].dtype)
    return out
```

```python
from contextlib import ExitStack

import numpy as np
import concourse.bass as bass
from concourse import mybir

F32 = mybir.dt.float32
F32R = mybir.dt.float32r
BF16 = mybir.dt.bfloat16
I32 = mybir.dt.int32
U32 = mybir.dt.uint32
ALU = mybir.AluOpType
ACT = mybir.ActivationFunctionType
AX = mybir.AxisListType

P = 128
D = 1024
C = D // P
S = 256
TT = S // P
DEPTH = 2
FF = 2816
EF = 3584
GW = 256
FG = FF // GW
EG = EF // GW
E = 8
IN_W = 3488
TILE = C * GW
RAW = 6
SPLIT = 3
EPS = 1e-6
HALF = 512

LAYER_VECS = [("ffn1_norm", 8), ("mix_norm", 8), ("ffn2_norm", 8), ("conv_w", 6), ("rwkv_w0_f", 2),
              ("rwkv_w0_b", 2), ("rwkv_a0_f", 2), ("rwkv_a0_b", 2), ("rwkv_k_k", 2), ("rwkv_k_a", 2),
              ("rwkv_r_k", 2), ("rwkv_lnx_g", 2), ("rwkv_lnx_b", 2), ("ret_gn_g", 2),
              ("mla_q_a_norm", 3), ("mla_kv_a_norm", 1)]
LV = {}
_at = 0
for _name, _n in LAYER_VECS:
    LV[_name] = _at
    _at += _n
NLV = _at
SECOND_VECS = [("norm_mix_g_2", 16), ("norm_ffn_g_2", 16), ("dn_norm_g_2", 1), ("dn_conv_w_2", 96)]
SV = {}
_at = 0
for _name, _n in SECOND_VECS:
    SV[_name] = _at
    _at += _n
NSV = _at

CONST = {}
_cw = 0
for _name, _n in [("ident", 128), ("ones", 128), ("bdones", 128), ("stack", 64), ("low", 6 * 128),
                  ("up", 6 * 128), ("strict_low", 128), ("strict_up", 128), ("incl_low", 128),
                  ("incl_up", 128), ("rot64", 128), ("rot96", 96), ("reset", 256), ("inv", 2),
                  ("tri", 128), ("iota", 128), ("small", 16)]:
    CONST[_name] = (_cw, _n)
    _cw += _n
NCONST = _cw
SMALL = {"eps": 0, "gn_eps": 1, "half_pi": 2, "nope": 3, "zero": 4, "one": 5}


def constants():
    c = np.zeros((P, NCONST), np.float32)

    def put(name, a):
        s, n = CONST[name]
        c[:a.shape[0], s:s + n] = a

    i = np.arange(P)
    blk = (i[:, None] // 64 == i[None, :] // 64)
    put("ident", np.eye(P))
    put("ones", np.ones((P, P)))
    put("bdones", blk)
    put("stack", np.tile(np.eye(64), (2, 1)))
    low = []
    for b in (1, 2, 4, 8, 16, 32):
        low.append((i[:, None] // (2 * b) == i[None, :] // (2 * b)) & ((i[:, None] // b) % 2 == 1)
                   & ((i[None, :] // b) % 2 == 0))
    put("low", np.concatenate(low, 1))
    put("up", np.concatenate([m.T for m in low], 1))
    put("strict_low", blk & (i[:, None] > i[None, :]))
    put("strict_up", blk & (i[:, None] < i[None, :]))
    put("incl_low", blk & (i[:, None] >= i[None, :]))
    put("incl_up", blk & (i[:, None] <= i[None, :]))
    r = np.zeros((P, P))
    for h in range(2):
        for j in range(32):
            r[h * 64 + 32 + j, h * 64 + j] = -1
            r[h * 64 + j, h * 64 + 32 + j] = 1
    put("rot64", r)
    r = np.zeros((96, 96))
    for j in range(16):
        r[64 + 16 + j, 64 + j] = -1
        r[64 + j, 64 + 16 + j] = 1
    put("rot96", r)
    t = np.arange(S)
    put("reset", np.tile((t % 64 != 0)[None], (P, 1)))
    inv = np.zeros((P, 2), np.float32)
    inv[:, 0] = np.power(np.float32(10000.0), -(i % 32).astype(np.float32) / np.float32(32))
    inv[64:96, 1] = np.power(np.float32(10000.0), -((i[64:96] - 64) % 16).astype(np.float32) / np.float32(16))
    put("inv", inv)
    put("tri", i[:, None] < i[None, :])
    put("iota", np.tile(i[None], (P, 1)))
    sm = np.zeros((P, 16), np.float32)
    sm[:, SMALL["eps"]] = EPS
    sm[:, SMALL["gn_eps"]] = 64e-5
    sm[:, SMALL["half_pi"]] = np.pi / 2
    sm[:, SMALL["one"]] = 1.0
    put("small", sm)
    return c


def retention_decay():
    i = np.arange(S)
    g = np.log(1.0 - 2.0 ** (-5.0 - np.arange(4)))
    return np.exp(g[:, None, None] * np.abs(i[None, :, None] - i[None, None, :])).astype(np.float32)


def pool_counts():
    t = np.arange(1, S + 1)
    c = np.stack([1.0 / np.minimum(t, w) for w in (2, 4, 8, 16)])
    return np.tile(c[None], (P, 1, 1)).astype(np.float32)


FLAGS = ["arrived", "consts", "x_in", "vecs", "vecs_t", "squares", "norm_root", "scaled",
         "transposed", "norm_hi", "xt_ready", "pos_in", "angles", "rot", "roped", "decay_in", "ret_scores",
         "ret_decayed", "ret_o", "ret_sq", "ret_ms", "ret_rt", "mla_w", "mla_sq", "mla_ms", "mla_rt",
         "mla_normed", "qkv", "qk_copied", "mla_rot", "mla_roped", "mla_scores", "mla_max", "mla_exp",
         "probs_normed", "probs_tr", "probs_t", "mla_o",
         "rk_w", "rk_tanh", "rk_logits", "rk_sig", "rk_kk2", "rk_knorm", "rk_cums", "rk_exps", "rk_toks",
         "rk_toks_sb", "rk_var", "rk_std", "sol_LT", "sol_yps", "sol_Lm", "rk_kx", "rk_vbd", "rk_vps", "rk_bd",
         "sol_T", "sol_ysb", "sol_zps", "rk_S", "rk_rhs", "rk_rhs_sb", "rk_sa", "rk_sa_sb", "rk_sy", "rk_prod",
         "rk_bonus", "rk_ybd", "rk_yT",
         "pooled", "narrow_in", "narrow_hi", "narrow_lo", "narrow_done", "dn_z", "dn_sp", "dn_gc", "dn_eg",
         "dn_tail", "dn_conv", "dn_silu", "dn_sq", "dn_ss", "dn_rt", "dn_gr", "dn_unit", "dn_turned",
         "dn_taken", "dn_diag", "dn_gram", "dn_L", "dn_LT", "dn_dec", "dn_exp", "dn_S", "dn_ks", "dn_rhs",
         "dn_new", "dn_upd", "dn_ku", "dn_o", "dn_on", "dn_oT", "dn_om", "dn_or", "sel", "ranks", "top",
         "top_exp", "picked", "gathered", "gt", "ye", "back",
         "x_out"]
WORK = 10400


LAYER_PLAN = ['vectors', 'ffn1', 'proj', 'ret', 'mla', 'rwkv', 'out', 'ffn2']
SECOND_PLAN = ['final1', 'pool_in', 'pool', 'ffn3', 'dn_in', 'dn_pre', 'dn_chunk', 'dn_scan', 'dn_out', 'route', 'moe', 'final2']


def build(nc, a, out):
    with ExitStack() as ctx:
        def sb(name, shape, dt=F32):
            return ctx.enter_context(nc.sbuf_tensor(name, shape, dt))

        def sem(name):
            return ctx.enter_context(nc.semaphore(name))

        con = sb("con", [P, NCONST])
        x = sb("x", [P, TT, D])
        vec = sb("vec", [P, DEPTH * NLV + NSV])
        cur = sb("cur", [P, NLV])
        raw = sb("raw", [P, RAW, TILE])
        whi = sb("whi", [P, SPLIT, TILE], F32R)
        wlo = sb("wlo", [P, SPLIT, TILE], F32R)
        xhi = sb("xhi", [P, C, S], F32R)
        xlo = sb("xlo", [P, C, S], F32R)
        hhi = sb("hhi", [P, 2, 2, S], F32R)
        hlo = sb("hlo", [P, 2, 2, S], F32R)
        work = sb("work", [P, WORK])
        U = sb("U", [P, 32, S])
        rope = sb("rope", [P, 4, S])
        tiny = sb("tiny", [P, 128])
        dn_tiny = sb("dn_tiny", [P, 192])
        dn_rows = sb("dn_rows", [P, 16])
        nar = sb("nar", [P, C * 16])
        nar_hi = sb("nar_hi", [P, C * 16], F32R)
        nar_lo = sb("nar_lo", [P, C * 16], F32R)
        ids = sb("ids", [1, 16], I32)
        idx_u = sb("idx_u", [P, TT, E], U32)
        zero = sb("zero", [P, HALF], BF16)
        ps = ctx.enter_context(nc.psum_tensor("ps", [P, 8, HALF], F32))

        def const(name, lo=0, n=None, p=P):
            s, w = CONST[name]
            return con[0:p, s + lo:s + lo + (w if n is None else n)]

        def small(name, p=P):
            return const("small", SMALL[name], 1, p)

        sil = work[:, 0:2 * 512].rearrange("p (a b) -> p a b", a=2)
        hid = work[:, 1024:1536]
        xs = work[:, 1536:1536 + TT * D].rearrange("p (t d) -> p t d", t=TT)

        raw_landed = [sem(f"raw_landed{i}") for i in range(RAW)]
        raw_free = [sem(f"raw_free{i}") for i in range(RAW)]
        hi_ready = [sem(f"hi_ready{i}") for i in range(SPLIT)]
        split_ready = [sem(f"split_ready{i}") for i in range(SPLIT)]
        tile_done = [sem(f"tile_done{i}") for i in range(SPLIT)]
        hid_ready = [sem(f"hid_ready{i}") for i in range(2)]
        hid_made = [sem(f"hid_made{i}") for i in range(2)]
        hid_turned = [sem(f"hid_turned{i}") for i in range(2)]
        hid_hi = [sem(f"hid_hi{i}") for i in range(2)]
        go = {k: sem(f"go_{k}") for k in ("pe", "dve", "act")}
        items_ready = sem("items_ready")
        f = {k: sem(k) for k in FLAGS}
        flag_range = range(f[FLAGS[0]].num, f[FLAGS[-1]].num + 1)
        assert len(flag_range) == len(FLAGS)

        def take(eng, s, n=1):
            eng.wait_ge(s, n)
            eng.sem_clear(s)

        def section_end(eng, name):
            eng.drain().then_inc(f["arrived"], 1)
            take(eng, go[name])

        def section_end_pool(pool):
            pool.wait_ge(f["arrived"], 3)
            pool.sem_clear(flag_range)
            for k in go.values():
                pool.sem_inc(k, 1)

        def load_tile(sp, n, src):
            take(sp, raw_free[n % RAW])
            sp.dma_start(raw[:, n % RAW, 0:src.shape[1] * src.shape[2]]
                         .rearrange("p (c f) -> p c f", c=src.shape[1]), src).then_inc(raw_landed[n % RAW], 16)

        def cols(w, row0, col0, width=GW, blocks=C):
            return w[bass.ds(row0, blocks * P), bass.ds(col0, width)].rearrange("(c p) f -> p c f", p=P)

        def split_hi(act, n, width=TILE):
            act.wait_ge(raw_landed[n % RAW], 16)
            act.sem_clear(raw_landed[n % RAW])
            act.copy(whi[:, n % SPLIT, 0:width], raw[:, n % RAW, 0:width]).then_inc(hi_ready[n % SPLIT], 1)

        def split_lo(dve, n, width=TILE):
            dve.tensor_tensor(wlo[:, n % SPLIT, 0:width], raw[:, n % RAW, 0:width], whi[:, n % SPLIT, 0:width],
                              ALU.subtract).then_inc(split_ready[n % SPLIT], 1)
            dve.drain().then_inc(raw_free[n % RAW], 1)

        def ffn_stream(sp, n, wg, wu, wd, row0, frow0, groups):
            load_tile(sp, n, cols(wg, row0, 0))
            load_tile(sp, n + 1, cols(wu, row0, 0))

            def step(g, m):
                load_tile(sp, m, cols(wg, row0, g * GW))
                load_tile(sp, m + 1, cols(wu, row0, g * GW))
                load_tile(sp, m + 2, cols(wd, frow0 + (g - 1) * GW, 0, D, 2))
            n += 2
            pairs = (groups - 1) // 2
            with sp.Fori(0, pairs) as i:
                step(i * 2 + 1, n)
                step(i * 2 + 2, n + 3)
            if groups % 2 == 0:
                step(groups - 1, n)
            load_tile(sp, n + 3 * (groups - 1), cols(wd, frow0 + (groups - 1) * GW, 0, D, 2))

        def norm_scalar(act):
            for t in range(TT):
                act.activation(ps[:, 4:6, :].rearrange("p a b -> p (a b)"), x[:, t, :], ACT.Square,
                               accum_out=tiny[:, t:t + 1])
                act.drain()
            act.activation(tiny[:, 2:4], tiny[:, 0:2], ACT.Sqrt, bias=small("eps"),
                           scale=1.0 / D).then_inc(f["norm_root"], 1)

        def norm_gain_scalar(act, gain):
            for c in range(C):
                act.wait_ge(f["transposed"], c + 1)
                act.activation(xhi[:, c, :], ps[:, c, 0:S], ACT.Copy,
                               scale=gain(c)).then_inc(f["norm_hi"], 1)

        def norm_vector(dve, gain):
            dve.wait_ge(f["norm_root"], 1)
            dve.reciprocal(tiny[:, 4:6], tiny[:, 2:4])
            dve.drain()
            for t in range(TT):
                dve.tensor_scalar(xs[:, t, :], x[:, t, :], tiny[:, 4 + t:5 + t], None,
                                  ALU.mult).then_inc(f["scaled"], 1)
            for c in range(C):
                dve.wait_ge(f["norm_hi"], c + 1)
                dve.scalar_tensor_tensor(out=xlo[:, c, :], in0=ps[:, c, 0:S],
                                         scalar=gain(c), in1=xhi[:, c, :], op0=ALU.mult,
                                         op1=ALU.subtract).then_inc(f["xt_ready"], 1)

        def norm_tensor(pe):
            for t in range(TT):
                pe.wait_ge(f["scaled"], t + 1)
                for c in range(C):
                    tr = pe.transpose(ps[:, c, t * P:(t + 1) * P],
                                      xs[:, t, c * P:(c + 1) * P], const("ident"))
                    if t == TT - 1:
                        tr.then_inc(f["transposed"], 1)

        PASSES = ((whi, 0), (wlo, 0), (whi, 1))

        def take_split(pe, n):
            take(pe, split_ready[n % SPLIT])

        def wide(pe, n, dst, ntok, xt, fresh=False):
            if fresh:
                pe.wait_ge(f["xt_ready"], C)
            take_split(pe, n)
            for b in range(2):
                for c in range(C):
                    for k, (w, part) in enumerate(PASSES):
                        mm = pe.matmul(dst[:, b * ntok:(b + 1) * ntok],
                                       w[:, n % SPLIT, c * GW + b * P:c * GW + (b + 1) * P],
                                       xt[part][:, c, 0:ntok], start=(c == 0 and k == 0),
                                       stop=(c == C - 1 and k == 2))
            return mm

        def down(pe, n, hp, nt, last):
            take_split(pe, n)
            for b in range(2):
                for t in range(nt):
                    for s in range(2):
                        for k, (w, part) in enumerate(PASSES):
                            mm = pe.matmul(ps[:, 2 * t + s, :], hp[part][b][:, t * P:(t + 1) * P],
                                           w[:, n % SPLIT, b * D + s * HALF:b * D + (s + 1) * HALF],
                                           start=False, stop=(last and b == 1 and k == 2),
                                           skip_group_check=True)
            mm.then_inc(tile_done[n % SPLIT], 1)

        def open_y(pe, banks):
            for b in range(banks):
                pe.matmul(ps[:, b, :], zero[:, 0:P], zero[:, :], start=True, stop=False,
                          skip_group_check=True)

        def ffn_steps(eng, n, groups, step):
            pairs = (groups - 1) // 2
            with eng.Fori(0, pairs):
                step(n, 1)
                step(n + 3, 0)
            if groups % 2 == 0:
                step(n, 1)

        def hidden(q):
            return tuple([h[:, q, b, :] for b in range(2)] for h in (hhi, hlo))

        def ffn_tensor(pe, n, groups, nt=TT, after_norm=True):
            ntok = nt * P

            def gate_up(m, q, fresh=False):
                wide(pe, m, ps[:, 4 + q, :], ntok, (xhi, xlo), fresh).then_inc(tile_done[m % SPLIT], 1)
                wide(pe, m + 1, ps[:, 6 + q, :], ntok, (xhi, xlo)).then_inc(tile_done[(m + 1) % SPLIT], 1)

            def step(m, q):
                gate_up(m, q)
                take(pe, hid_ready[1 - q])
                down(pe, m + 2, hidden(1 - q), nt, False)

            gate_up(n, 0, after_norm)
            open_y(pe, 2 * nt)
            ffn_steps(pe, n + 2, groups, step)
            q = (groups - 1) % 2
            take(pe, hid_ready[q])
            down(pe, n + 3 * groups - 1, hidden(q), nt, True)

        def ffn_scalar(act, n, groups, nt=TT):
            w = 2 * nt * P

            def gate(m, q):
                take(act, tile_done[m % SPLIT])
                act.activation(sil[:, q, 0:w], ps[:, 4 + q, 0:w], ACT.Silu)
                split_hi(act, m + SPLIT)

            def other(m):
                take(act, tile_done[m % SPLIT])
                split_hi(act, m + SPLIT)

            def step(m, q):
                gate(m, q)
                other(m + 1)
                other(m + 2)

            gate(n, 0)
            other(n + 1)
            ffn_steps(act, n + 2, groups, step)
            other(n + 3 * groups - 1)

        def ffn_vector(dve, n, groups, nt=TT):
            w = 2 * nt * P
            ntok = nt * P

            def refill(m):
                take(dve, hi_ready[m % SPLIT])
                split_lo(dve, m)

            def hid_group(q):
                dve.tensor_tensor(hid[:, 0:w], ps[:, 6 + q, 0:w], sil[:, q, 0:w], ALU.mult)
                dve.drain()
                hv = hid[:, 0:w].rearrange("p (b t) -> p b t", b=2)
                dve.tensor_copy(hhi[:, q, :, 0:ntok], hv)
                dve.drain()
                dve.tensor_tensor(hlo[:, q, :, 0:ntok], hv, hhi[:, q, :, 0:ntok],
                                  ALU.subtract).then_inc(hid_ready[q], 1)

            def step(m, q):
                refill(m + SPLIT)
                refill(m + 1 + SPLIT)
                hid_group(q)
                refill(m + 2 + SPLIT)

            refill(n + SPLIT)
            refill(n + 1 + SPLIT)
            hid_group(0)
            ffn_steps(dve, n + 2, groups, step)
            refill(n + 3 * groups - 1 + SPLIT)

        def add_y(dve, scale):
            for t in range(TT):
                for s in range(2):
                    xv = x[:, t, s * HALF:(s + 1) * HALF]
                    dve.scalar_tensor_tensor(out=xv, in0=ps[:, 2 * t + s, :], scalar=scale, in1=xv,
                                             op0=ALU.mult, op1=ALU.add)

        vrows = work[:, 0:3 * P].rearrange("p (k n) -> p k n", k=3)

        def start_sync(sp):
            sp.dma_start(con[:, :], a["consts"]).then_inc(f["consts"], 16)
            sp.dma_start(work[:, 1300:1556].bitcast(I32), a["positions"].rearrange("o t -> (o t)").partition_broadcast(P)) \
              .then_inc(f["pos_in"], 16)
            sp.dma_start(x[:, :, :], a["x"].rearrange("o (t p) d -> p (o t) d", p=P)).then_inc(f["x_in"], 16)
            for l in range(DEPTH):
                for name, n in LAYER_VECS:
                    src = a[name]
                    v = src[l:l + 1]
                    if len(v.shape) == 3:
                        v = v.rearrange("a b c -> a (b c)")
                    row = l * NLV + LV[name]
                    sp.dma_start(vrows[row:row + n, 0, :], v.rearrange("a (n q) -> (a n) q", q=P)).then_inc(f["vecs"], 16)
            for name, n in SECOND_VECS:
                v = a[name]
                if len(v.shape) == 3:
                    v = v.rearrange("a b c -> a (b c)")
                v = v.rearrange("a (n q) -> (a n) q", q=P)
                row = 0
                while row < n:
                    at = SV[name] + row
                    k, r = at // P, at % P
                    m = min(n - row, P - r)
                    sp.dma_start(vrows[r:r + m, 1 + k, :], v[row:row + m, :]).then_inc(f["vecs"], 16)
                    row += m

        def n_vec_loads():
            n = DEPTH * len(LAYER_VECS)
            for name, k in SECOND_VECS:
                n += 1 + ((SV[name] + k - 1) // P - SV[name] // P)
            return n

        VEC_ROWS = ((0, DEPTH * NLV, 0), (1, P, DEPTH * NLV), (2, NSV - P, DEPTH * NLV + P))

        def start_tensor(pe):
            pe.wait_ge(f["consts"], 16)
            pe.wait_ge(f["vecs"], 16 * n_vec_loads())
            for k, rows, at in VEC_ROWS:
                pe.transpose(ps[:, k, 0:rows], vrows[0:rows, k, :], const("ident", p=rows, n=rows)) \
                  .then_inc(f["vecs_t"], 1)
            for i in range(SPLIT):
                pe.sem_inc(tile_done[i], 1)

        def start_vector(dve):
            dve.memset(zero[:, :], 0.0)
            for k, rows, at in VEC_ROWS:
                dve.wait_ge(f["vecs_t"], k + 1)
                dve.tensor_copy(vec[:, at:at + rows], ps[:, k, 0:rows])
            rope_tables_vector(dve)
            for i in range(RAW):
                dve.sem_inc(raw_free[i], 1)
            for i in range(SPLIT):
                take(dve, hi_ready[i])
                split_lo(dve, i)

        def start_scalar(act):
            for i in range(SPLIT):
                take(act, tile_done[i])
                split_hi(act, i)
            rope_tables_scalar(act)
            act.wait_ge(f["x_in"], 16)

        def layer_vec(name):
            return lambda c: cur[:, LV[name] + c:LV[name] + c + 1]

        def second_vec(name, first=0):
            at = DEPTH * NLV + SV[name] + first
            return lambda c: vec[:, at + c:at + c + 1]

        COS64, SIN64, COS96, SIN96 = range(4)

        def rope_tables_vector(dve):
            pos = work[:, 400:656]
            ang = work[:, 700:956]
            turns = work[:, 1000:1256]
            dve.wait_ge(f["pos_in"], 16)
            dve.wait_ge(f["consts"], 16)
            dve.tensor_copy(pos, work[:, 1300:1556].bitcast(I32))
            dve.drain()
            for k, shift in ((COS64, 0.25), (SIN64, 0.0), (COS96, 0.25), (SIN96, 0.0)):
                magic = 1.5 * 2.0 ** 23
                dve.tensor_scalar(ang, pos, const("inv", k // 2, 1), None, ALU.mult)
                dve.drain()
                dve.tensor_scalar(turns, ang, float(1 / (2 * np.pi)), shift, ALU.mult, ALU.add)
                dve.drain()
                dve.tensor_scalar(turns, turns, magic, None, ALU.add)
                dve.drain()
                dve.tensor_scalar(turns, turns, magic, None, ALU.subtract)
                dve.drain()
                for part in (6.28125, float(2 * np.pi - 6.28125)):
                    dve.scalar_tensor_tensor(out=ang, in0=turns, scalar=-part, in1=ang, op0=ALU.mult,
                                             op1=ALU.add)
                    dve.drain()
                if shift:
                    dve.tensor_scalar(ang, ang, float(np.pi / 2), None, ALU.add)
                    dve.drain()
                dve.tensor_scalar(rope[:, k, :], ang, 3.1415925, -3.1415925, ALU.min, ALU.max)
                dve.drain()
            dve.drain().then_inc(f["angles"], 1)

        def rope_tables_scalar(act):
            act.wait_ge(f["angles"], 1)
            act.activation(rope[:, :, :], rope[:, :, :], ACT.Sin)

        U_CX, U_CB, U_CC, U_R, U_K, U_V, U_WD, U_AD, U_GD = 0, 2, 4, 6, 8, 10, 12, 13, 14
        U_RQ, U_RK, U_RV, U_RG, U_QA, U_CKV, U_KR = 15, 17, 19, 21, 23, 26, 27
        IN_TILES = -(-IN_W // GW)

        def tile_width(j, total):
            return min(GW, total - j * GW)

        def project_stream(sp, n, wt, row0, total):
            for j in range(-(-total // GW)):
                load_tile(sp, n + j, cols(wt, row0, j * GW, tile_width(j, total)))

        def project_tile(pe, n, width, starts, token_major=()):
            take_split(pe, n)
            for b, (at, m) in enumerate(starts):
                bank = 2 * (n % SPLIT) + b
                for c in range(C):
                    for k, (wp, part) in enumerate(PASSES):
                        xt = (xhi, xlo)[part]
                        wv = wp[:, n % SPLIT, c * width + at:c * width + at + m]
                        first, last = c == 0 and k == 0, c == C - 1 and k == 2
                        if b in token_major:
                            for t in range(TT):
                                mm = pe.matmul(ps[:, bank, t * P:(t + 1) * P], xt[:, c, t * P:(t + 1) * P], wv,
                                               start=first and t == 0, stop=last, skip_group_check=True)
                        else:
                            mm = pe.matmul(ps[0:m, bank, 0:S], wv, xt[:, c, :], start=first, stop=last)
            mm.then_inc(tile_done[n % SPLIT], 1)

        def project_tensor(pe, n, total, starts=lambda j: ((0, P), (P, P)), token_major=lambda j: ()):
            pe.wait_ge(f["xt_ready"], C)
            for j in range(-(-total // GW)):
                project_tile(pe, n + j, tile_width(j, total), starts(j), token_major(j))

        def project_scalar(act, n, total, dst, width=lambda j: TILE):
            for j in range(-(-total // GW)):
                m = n + j
                take(act, tile_done[m % SPLIT])
                act.copy(dst[:, 2 * j, :], ps[:, 2 * (m % SPLIT), 0:S])
                split_hi(act, m + SPLIT, width(j + SPLIT))

        def project_vector(dve, n, total, dst, rows=lambda j: slice(0, P), width=lambda j: TILE):
            for j in range(-(-total // GW)):
                m = n + j
                take(dve, hi_ready[m % SPLIT])
                dve.tensor_copy(dst[rows(j), 2 * j + 1, :], ps[rows(j), 2 * (m % SPLIT) + 1, 0:S])
                split_lo(dve, m + SPLIT, width(j + SPLIT))

        def in_starts(j):
            return ((0, P), (P, P)) if j < IN_TILES - 1 else ((0, P), (64, 96))

        def in_token_major(j):
            return {9: (1,), 10: (0,)}.get(j, ())

        def in_width(j):
            return C * tile_width(j, IN_W) if j < IN_TILES else TILE

        def add_project():
            def stream(sp, n, l):
                project_stream(sp, n, w["w_in"], l * D, IN_W)
                return n + IN_TILES

            def tensor(pe, n, l):
                norm_tensor(pe)
                project_tensor(pe, n, IN_W, in_starts, in_token_major)
                return n + IN_TILES

            def scalar(act, n, l):
                norm_scalar(act)
                norm_gain_scalar(act, layer_vec("mix_norm"))
                project_scalar(act, n, IN_W, U, in_width)
                return n + IN_TILES

            def vector(dve, n, l):
                norm_vector(dve, layer_vec("mix_norm"))
                project_vector(dve, n, IN_W, U, lambda j: slice(0, P if j < IN_TILES - 1 else 96), in_width)
                return n + IN_TILES
            STREAM["proj"], TENSOR["proj"], VECTOR["proj"], SCALAR["proj"] = stream, tensor, vector, scalar

        def add_out(part, name, row0=lambda l: l * D):
            tiles = C // 2

            def stream(sp, n, l):
                for j in range(tiles):
                    load_tile(sp, n + j, cols(w[name], row0(l) + 2 * j * P, 0, D, 2))
                return n + tiles

            def tensor(pe, n, l):
                open_y(pe, 2 * TT)
                for j in range(tiles):
                    down(pe, n + j, tuple([h[:, 2 * j + b, :] for b in range(2)] for h in (xhi, xlo)), TT,
                         j == tiles - 1)
                return n + tiles

            def scalar(act, n, l):
                for j in range(tiles):
                    take(act, tile_done[(n + j) % SPLIT])
                    split_hi(act, n + j + SPLIT)
                return n + tiles

            def vector(dve, n, l):
                for j in range(tiles):
                    take(dve, hi_ready[(n + j) % SPLIT])
                    split_lo(dve, n + j + SPLIT)
                add_y(dve, 1.0)
                return n + tiles
            STREAM[part], TENSOR[part], VECTOR[part], SCALAR[part] = stream, tensor, vector, scalar

        def put_y(dve, c, src):
            dve.tensor_copy(xhi[:, c, :], src)
            dve.drain()
            dve.tensor_tensor(xlo[:, c, :], src, xhi[:, c, :], ALU.subtract)

        decay = work[:, 0:2048].rearrange("p (h t i) -> p h t i", h=4, t=2)
        ret_s = work[:, 2048:4096].rearrange("p (h t i) -> p h t i", h=4, t=2)
        ret_tmp = work[:, 4096:5120].rearrange("p (a i) -> p a i", a=4)
        cu = work[:, 5120:5632].rearrange("p (b t) -> p b t", b=2)
        cy = work[:, 5632:6144].rearrange("p (b t) -> p b t", b=2)
        ret_sq = work[:, 6144:6656].rearrange("p (b t) -> p b t", b=2)
        ret_rt = work[:, 6656:7168].rearrange("p (b t) -> p b t", b=2)
        ret_g = work[:, 7168:7680].rearrange("p (b t) -> p b t", b=2)

        def bc(ap, n):
            p, t = ap.shape
            return ap.unsqueeze(1).to_broadcast([p, n, t])

        def conv_vector(dve):
            def cw(k, b):
                return layer_vec("conv_w")(2 * k + b)
            dve.tensor_tensor(cu, U[:, U_CX:U_CX + 2, :], U[:, U_CC:U_CC + 2, :], ALU.mult)
            dve.drain()
            for b in range(2):
                dve.tensor_scalar(cy[:, b, :], cu[:, b, :], cw(1, b), None, ALU.mult)
            dve.drain()
            for b in range(2):
                dve.scalar_tensor_tensor(out=cy[:, b, 1:S], in0=cu[:, b, 0:S - 1], scalar=cw(0, b),
                                         in1=cy[:, b, 1:S], op0=ALU.mult, op1=ALU.add)
            dve.drain()
            for b in range(2):
                dve.scalar_tensor_tensor(out=cy[:, b, 0:S - 1], in0=cu[:, b, 1:S], scalar=cw(2, b),
                                         in1=cy[:, b, 0:S - 1], op0=ALU.mult, op1=ALU.add)
            dve.drain()
            dve.tensor_tensor(cy, cy, U[:, U_CB:U_CB + 2, :], ALU.mult)
            dve.drain()
            for b in range(2):
                put_y(dve, b, cy[:, b, :])

        def ret_tensor(pe):
            for i in range(4):
                mm = pe.matmul(ps[:, i, 0:S], const("rot64"), U[:, U_RQ + i, :], start=True, stop=True)
            mm.then_inc(f["rot"], 1)
            pe.wait_ge(f["roped"], 1)
            for h in range(4):
                r = slice(64 * (h % 2), 64 * (h % 2) + 64)
                for t in range(TT):
                    mm = pe.matmul(ps[:, 4 + h, t * S:(t + 1) * S], U[r, U_RK + h // 2, t * P:(t + 1) * P],
                                   U[r, U_RQ + h // 2, :], start=True, stop=True)
                mm.then_inc(f["ret_scores"], 1)
            for h in range(4):
                pe.wait_ge(f["ret_decayed"], h + 1)
                r = slice(64 * (h % 2), 64 * (h % 2) + 64)
                for t in range(TT):
                    v = U[:, U_RV + h // 2, :].rearrange("p (t f) -> p t f", t=TT)[:, t, r]
                    mm = pe.matmul(ps[r, h // 2, 0:S], v, ret_s[:, h, t, :], start=(t == 0), stop=(t == TT - 1))
                if h % 2:
                    mm.then_inc(f["ret_o"], 1)
            pe.wait_ge(f["ret_sq"], 1)
            for b in range(2):
                mm = pe.matmul(ps[:, 2 + b, 0:S], const("bdones"), ret_sq[:, b, :], start=True, stop=True)
            mm.then_inc(f["ret_ms"], 1)

        def ret_scalar(act):
            act.dma_start(decay, a["decay"].rearrange("h (t p) i -> p h t i", p=P)).then_inc(f["decay_in"], 16)
            act.activation(ret_g, U[:, U_RG:U_RG + 2, :], ACT.Silu)
            act.wait_ge(f["ret_o"], 2)
            act.activation(ret_sq, ps[:, 0:2, 0:S], ACT.Square).then_inc(f["ret_sq"], 1)
            act.wait_ge(f["ret_ms"], 1)
            act.activation(ret_rt, ps[:, 2:4, 0:S], ACT.Sqrt, bias=small("eps"), scale=1.0 / 64) \
               .then_inc(f["ret_rt"], 1)

        def ret_vector(dve):
            q = U[:, U_RQ:U_RQ + 4, :]
            dve.wait_ge(f["rot"], 1)
            dve.tensor_tensor(ret_tmp, ps[:, 0:4, 0:S], bc(rope[:, SIN64, :], 4), ALU.mult)
            dve.tensor_tensor(q, q, bc(rope[:, COS64, :], 4), ALU.mult)
            dve.drain()
            dve.tensor_tensor(q, q, ret_tmp, ALU.add).then_inc(f["roped"], 1)
            dve.wait_ge(f["decay_in"], 16)
            for h in range(4):
                dve.wait_ge(f["ret_scores"], h + 1)
                dve.scalar_tensor_tensor(out=ret_s[:, h, :, :], in0=ps[:, 4 + h, :].rearrange("p (t i) -> p t i", t=TT),
                                         scalar=64 ** -0.5, in1=decay[:, h, :, :], op0=ALU.mult,
                                         op1=ALU.mult).then_inc(f["ret_decayed"], 1)
            conv_vector(dve)
            dve.wait_ge(f["ret_rt"], 1)
            dve.reciprocal(ret_rt, ret_rt)
            dve.drain()
            dve.tensor_tensor(ret_rt, ret_rt, ret_g, ALU.mult)
            dve.drain()
            for b in range(2):
                dve.scalar_tensor_tensor(out=ret_tmp[:, b, :], in0=ps[:, b, 0:S], scalar=layer_vec("ret_gn_g")(b),
                                         in1=ret_rt[:, b, :], op0=ALU.mult, op1=ALU.mult)
            dve.drain()
            for b in range(2):
                put_y(dve, 4 + b, ret_tmp[:, b, :])

        QD = 96
        mla_sq = work[:, 0:1024].rearrange("p (b t) -> p b t", b=4)
        mla_rt = work[:, 1024:1536].rearrange("p (b t) -> p b t", b=2)
        mla_qb = work[:, 1536:2688].rearrange("p (c n) -> p c n", c=3)
        mla_kvb = work[:, 2688:3200]
        Q = work[:, 3200:4224].rearrange("p (h t) -> p h t", h=4)
        K = work[:, 4224:5248].rearrange("p (h t) -> p h t", h=4)
        mla_v = work[:, 5248:5760].rearrange("p (t n) -> p t n", t=TT)
        mla_tmp = work[:, 5760:6784].rearrange("p (h t) -> p h t", h=4)
        probs = work[:, 6784:8832].rearrange("p (h t k) -> p h t k", h=4, t=TT)
        probs_t = work[:, 0:1024].rearrange("p (h k q) -> p h k q", h=2, k=TT)
        probs_t2 = work[:, 8832:9856].rearrange("p (h k q) -> p h k q", h=2, k=TT)

        def pt(h):
            return (probs_t if h < 2 else probs_t2)[:, h % 2, :, :]

        def mla_scalar(act, l):
            act.dma_start(mla_qb, flat2(a["mla_q_b"])[bass.ds(l * 384, 384), :]
                          .rearrange("(c p) n -> p c n", p=P)).then_inc(f["mla_w"], 16)
            act.dma_start(mla_kvb, flat2(a["mla_kv_b"])[bass.ds(l * P, P), :]).then_inc(f["mla_w"], 16)
            act.activation(mla_sq, U[:, U_QA:U_QA + 4, :], ACT.Square).then_inc(f["mla_sq"], 1)
            act.wait_ge(f["mla_ms"], 1)
            for b, n in ((0, 384), (1, P)):
                rt = act.activation(mla_rt[:, b, :], ps[:, b, 0:S], ACT.Sqrt, bias=small("eps"), scale=1.0 / n)
            rt.then_inc(f["mla_rt"], 1)
            act.wait_ge(f["mla_max"], 1)
            for h in range(4):
                for t in range(TT):
                    i = 2 * h + t
                    e = act.activation(probs[:, h, t, :], ps[:, h, t * S:(t + 1) * S], ACT.Exp,
                                       bias=tiny[:, 16 + i:17 + i], scale=QD ** -0.5, accum_out=tiny[:, 24 + i:25 + i])
                e.then_inc(f["mla_exp"], 1)
            for h in range(4):
                act.wait_ge(f["probs_tr"], h + 1)
                act.copy(pt(h), ps[:, 4 + h, :].rearrange("p (k q) -> p k q", k=TT)).then_inc(f["probs_t"], 1)

        def mla_tensor(pe):
            pe.wait_ge(f["mla_sq"], 1)
            for c in range(3):
                pe.matmul(ps[:, 0, 0:S], const("ones"), mla_sq[:, c, :], start=(c == 0), stop=(c == 2))
            pe.matmul(ps[:, 1, 0:S], const("ones"), mla_sq[:, 3, :], start=True, stop=True).then_inc(f["mla_ms"], 1)
            pe.wait_ge(f["mla_w"], 32)
            pe.wait_ge(f["mla_normed"], 1)
            for h in range(4):
                for c in range(3):
                    pe.matmul(ps[0:QD, h, 0:S], mla_qb[:, c, h * QD:(h + 1) * QD], U[:, U_QA + c, :],
                              start=(c == 0), stop=(c == 2))
                pe.matmul(ps[0:64, 4 + h // 2, (h % 2) * S:(h % 2 + 1) * S], mla_kvb[:, h * P:h * P + 64],
                          U[:, U_CKV, :], start=True, stop=True)
            for t in range(TT):
                mm = pe.matmul(ps[:, 6, t * S:(t + 1) * S], U[:, U_CKV, t * P:(t + 1) * P],
                               mla_kvb.rearrange("p (h a d) -> p h a d", h=4, a=2)[:, :, 1, :], start=True, stop=True)
            mm.then_inc(f["qkv"], 1)
            pe.wait_ge(f["qk_copied"], 1)
            for h in range(4):
                pe.matmul(ps[0:QD, h, 0:S], const("rot96", p=QD), Q[0:QD, h, :], start=True, stop=True)
            pe.matmul(ps[0:QD, 7, 0:S], const("rot96", p=QD), K[0:QD, 0, :], start=True, stop=True) \
              .then_inc(f["mla_rot"], 1)
            pe.wait_ge(f["mla_roped"], 1)
            for h in range(4):
                for t in range(TT):
                    mm = pe.matmul(ps[:, h, t * S:(t + 1) * S], Q[0:QD, h, t * P:(t + 1) * P], K[0:QD, h, :],
                                   start=True, stop=True)
            mm.then_inc(f["mla_scores"], 1)
            for h in range(4):
                pe.wait_ge(f["probs_normed"], h + 1)
                for k in range(TT):
                    for t in range(TT):
                        tr = pe.transpose(ps[:, 4 + h, k * S + t * P:k * S + (t + 1) * P],
                                          probs[:, h, t, k * P:(k + 1) * P], const("ident"))
                tr.then_inc(f["probs_tr"], 1)
            for h in range(4):
                pe.wait_ge(f["probs_t"], h + 1)
                r = slice(64 * (h % 2), 64 * (h % 2) + 64)
                for k in range(TT):
                    mm = pe.matmul(ps[r, h // 2, 0:S], mla_v[:, k, h * 64:(h + 1) * 64], pt(h)[:, k, :],
                                   start=(k == 0), stop=(k == TT - 1))
            mm.then_inc(f["mla_o"], 1)

        def mla_vector(dve):
            dve.wait_ge(f["mla_rt"], 1)
            dve.reciprocal(mla_rt, mla_rt)
            dve.drain()
            for c in range(4):
                gain = layer_vec("mla_q_a_norm")(c) if c < 3 else layer_vec("mla_kv_a_norm")(0)
                st = dve.scalar_tensor_tensor(out=U[:, U_QA + c, :], in0=U[:, U_QA + c, :], scalar=gain,
                                              in1=mla_rt[:, c // 3, :], op0=ALU.mult, op1=ALU.mult)
            st.then_inc(f["mla_normed"], 1)
            dve.wait_ge(f["qkv"], 1)
            dve.tensor_copy(Q[0:QD, :, :], ps[0:QD, 0:4, 0:S])
            dve.tensor_copy(K[0:64, :, :], ps[0:64, 4:6, :].rearrange("p b (h t) -> p (b h) t", h=2))
            dve.tensor_copy(mla_v, ps[:, 6, :].rearrange("p (t n) -> p t n", t=TT))
            dve.tensor_copy(K[64:QD, :, :], bc(U[64:QD, U_KR, :], 4))
            dve.drain().then_inc(f["qk_copied"], 1)
            dve.wait_ge(f["mla_rot"], 1)
            dve.tensor_tensor(mla_tmp[0:QD, :, :], ps[0:QD, 0:4, 0:S], bc(rope[0:QD, SIN96, :], 4), ALU.mult)
            dve.tensor_tensor(Q[0:QD, :, :], Q[0:QD, :, :], bc(rope[0:QD, COS96, :], 4), ALU.mult)
            dve.drain()
            dve.tensor_tensor(Q[0:QD, :, :], Q[0:QD, :, :], mla_tmp[0:QD, :, :], ALU.add)
            dve.drain()
            kr = mla_tmp[64:QD, 0, :]
            dve.tensor_tensor(kr, ps[64:QD, 7, 0:S], rope[64:QD, SIN96, :], ALU.mult)
            dve.tensor_tensor(U[64:QD, U_KR, :], U[64:QD, U_KR, :], rope[64:QD, COS96, :], ALU.mult)
            dve.drain()
            dve.tensor_tensor(K[64:QD, :, :], bc(U[64:QD, U_KR, :], 4), bc(kr, 4), ALU.add)
            dve.drain().then_inc(f["mla_roped"], 1)
            dve.wait_ge(f["mla_scores"], 1)
            dve.tensor_reduce(tiny[:, 8:16], ps[:, 0:4, :].rearrange("p h (t k) -> p (h t) k", t=TT), AX.X, ALU.max)
            dve.drain()
            dve.tensor_scalar(tiny[:, 16:24], tiny[:, 8:16], -QD ** -0.5, None, ALU.mult).then_inc(f["mla_max"], 1)
            for h in range(4):
                dve.wait_ge(f["mla_exp"], h + 1)
                dve.reciprocal(tiny[:, 32 + 2 * h:34 + 2 * h], tiny[:, 24 + 2 * h:26 + 2 * h])
                dve.drain()
                for t in range(TT):
                    i = 2 * h + t
                    sc = dve.tensor_scalar(probs[:, h, t, :], probs[:, h, t, :], tiny[:, 32 + i:33 + i], None, ALU.mult)
                sc.then_inc(f["probs_normed"], 1)
            dve.wait_ge(f["mla_o"], 1)
            for b in range(2):
                put_y(dve, 6 + b, ps[:, b, 0:S])

        LEVELS = 5

        def four(bank):
            return ps[:, bank, :].rearrange("p (c m) -> p c m", c=4)

        def solve_pool(pool, u, LT, Lm, masks):
            pool.wait_ge(f["sol_LT"], u + 1)
            for lv in range(LEVELS):
                if lv >= 2:
                    pool.wait_ge(f["sol_yps"], u * LEVELS + lv - 1)
                pool.tensor_tensor(Lm[lv % 2], LT, bc(const(masks, (lv + 1) * P, P), 4), ALU.mult) \
                    .then_inc(f["sol_Lm"], 1)

        def solve_tensor(pe, u, Lm, T, TT, Y):
            for lv in range(LEVELS):
                i = u * LEVELS + lv
                pe.wait_ge(f["sol_T"], i + 1)
                pe.wait_ge(f["sol_Lm"], i + 1)
                for c in range(4):
                    mm = pe.matmul(ps[:, 7, c * P:(c + 1) * P], Lm[lv % 2][:, c, :], T[:, c, :], start=True, stop=True)
                mm.then_inc(f["sol_yps"], 1)
                pe.wait_ge(f["sol_ysb"], i + 1)
                if lv < LEVELS - 1:
                    for c in range(4):
                        pe.matmul(ps[:, 0, c * P:(c + 1) * P], TT[:, c, :], Y[:, c, :], start=True, stop=True)
                for c in range(4):
                    mm = pe.matmul(ps[:, 5, c * P:(c + 1) * P], Y[:, c, :], TT[:, c, :], start=True, stop=True)
                mm.then_inc(f["sol_zps"], 1)

        def solve_start_vector(dve, L, LT, T, TT, lo, up):
            dve.tensor_tensor(T, L, bc(const(lo, 0, P), 4), ALU.mult)
            dve.drain()
            dve.tensor_tensor(TT, LT, bc(const(up, 0, P), 4), ALU.mult)
            dve.tensor_tensor(T, T, bc(const("ident"), 4), ALU.add)
            dve.drain()
            dve.tensor_tensor(TT, TT, bc(const("ident"), 4), ALU.add).then_inc(f["sol_T"], 1)

        def solve_vector(dve, u, T, TT, Y):
            for lv in range(LEVELS):
                i = u * LEVELS + lv
                dve.wait_ge(f["sol_yps"], i + 1)
                dve.tensor_copy(Y, four(7)).then_inc(f["sol_ysb"], 1)
                dve.wait_ge(f["sol_zps"], i + 1)
                if lv < LEVELS - 1:
                    dve.tensor_tensor(T, T, four(0), ALU.add)
                dve.tensor_tensor(TT, TT, four(5), ALU.add)
                if lv < LEVELS - 1:
                    dve.drain().then_inc(f["sol_T"], 1)

        CH = 64
        NC = S // CH
        KAPPA = float(np.exp(-0.5))
        UNITS = [(d, b) for d in range(2) for b in range(2)]
        U_flat = U.rearrange("p b t -> p (b t)")
        free = [[work, 0, WORK], [U_flat, U_RQ * S, 32 * S], [U_flat, 0, U_R * S]]
        def carve(n, shape):
            place = next(p for p in free if p[1] + n <= p[2])
            v = place[0][:, place[1]:place[1] + n]
            place[1] += n
            return v if shape is None else v.rearrange(shape[0], **shape[1])

        B2 = ("p (b t) -> p b t", {"b": 2})
        CH4 = ("p (c m) -> p c m", {"c": NC})
        rk_kk = carve(512, B2)
        rk_ksum = carve(512, B2)
        rk_sg = [carve(512, B2) for _ in range(2)]
        rk_a = [carve(512, B2) for _ in range(2)]
        rk_cum = carve(512, B2)
        rk_exc = carve(512, B2)
        rk_kd = carve(512, B2)
        rk_ab = carve(512, B2)
        rk_ei, rk_ee, rk_ev = (carve(512, B2) for _ in range(3))
        rk_tot = carve(2 * NC, ("p (b c) -> p b c", {"b": 2}))
        bd_ar = carve(2 * 512, ("p (c k m) -> p c k m", {"c": NC, "k": 2}))
        bd_b = carve(512, CH4)
        bd_k = carve(512, CH4)
        rk_T, rk_TT, rk_LT, rk_Y = (carve(512, CH4) for _ in range(4))
        rk_Lm = [carve(512, CH4) for _ in range(2)]
        rk_MK, rk_RB, rk_RK, rk_Bt, rk_Kt = (carve(512, CH4) for _ in range(5))
        rk_V = carve(2 * NC * 64, ("p (b c v) -> p b c v", {"b": 2, "c": NC}))
        rk_y = carve(2 * NC * 64, ("p (b c v) -> p b c v", {"b": 2, "c": NC}))
        rk_S = carve(64, None)
        rk_rhs = carve(64, None)
        rk_sa = carve(64, None)
        rk_w2 = rk_MK.rearrange("p c m -> p (c m)")[:, 0:256]
        rk_a2 = rk_MK.rearrange("p c m -> p (c m)")[:, 256:512]
        rk_g2 = carve(256, None)
        rk_omka = carve(2, None)
        rk_g = rk_sg[0]

        def half(ap4, hh):
            r = slice(hh * 64, hh * 64 + 64)
            return ap4[r, :, r]

        def chunks(ap, hh):
            return ap[hh * 64:hh * 64 + 64, :].rearrange("p (c t) -> p c t", c=NC)

        def rk_scalar(act, l):
            for dst, names in ((rk_w2, ("rwkv_w2_f", "rwkv_w2_b")), (rk_a2, ("rwkv_a2_f", "rwkv_a2_b"))):
                for d, name in enumerate(names):
                    act.dma_start(dst[d * 64:d * 64 + 64, :], flat2(a[name])[bass.ds(l * 64, 64), :]) \
                       .then_inc(f["rk_w"], 16)
            act.dma_start(rk_g2, flat2(a["rwkv_g2"])[bass.ds(l * P, P), :]).then_inc(f["rk_w"], 16)
            act.activation(U[:, U_WD, :], U[:, U_WD, :], ACT.Tanh)
            act.activation(U[:, U_GD, :], U[:, U_GD, :], ACT.Sigmoid).then_inc(f["rk_tanh"], 1)
            act.wait_ge(f["rk_logits"], 1)
            for d in range(2):
                for b in range(2):
                    act.activation(rk_sg[d][:, b, :], ps[:, 2 * d + b, 0:S], ACT.Sigmoid,
                                   bias=layer_vec(("rwkv_w0_f", "rwkv_w0_b")[d])(b))
                    sg = act.activation(rk_a[d][:, b, :], ps[:, 4 + 2 * d + b, 0:S], ACT.Sigmoid,
                                        bias=layer_vec(("rwkv_a0_f", "rwkv_a0_b")[d])(b))
            sg.then_inc(f["rk_sig"], 1)
            act.wait_ge(f["rk_kk2"], 1)
            act.activation(rk_ei, ps[:, 0:2, 0:S], ACT.Sqrt).then_inc(f["rk_knorm"], 1)
            for d in range(2):
                act.wait_ge(f["rk_cums"], d + 1)
                act.activation(rk_ei, rk_cum, ACT.Exp, scale=-KAPPA)
                act.activation(rk_ev, rk_cum, ACT.Exp, scale=KAPPA)
                act.activation(rk_ee, rk_exc, ACT.Exp, scale=-KAPPA)
                act.activation(rk_tot, rk_tot, ACT.Exp, scale=-KAPPA).then_inc(f["rk_exps"], 1)
                for b in range(2):
                    u = 2 * d + b
                    act.wait_ge(f["rk_toks"], u + 1)
                    act.copy(rk_Bt, ps[:, 5, :].rearrange("p (c m) -> p c m", c=NC))
                    act.copy(rk_Kt, ps[:, 6, :].rearrange("p (c m) -> p c m", c=NC)).then_inc(f["rk_toks_sb"], 1)
            act.wait_ge(f["rk_var"], 1)
            act.activation(tiny[:, 56:64], tiny[:, 48:56], ACT.Sqrt, bias=small("gn_eps"),
                           scale=1.0 / 64).then_inc(f["rk_std"], 1)

        def rk_pool(pool, l):
            for u, (d, b) in enumerate(UNITS):
                solve_pool(pool, u, rk_LT, rk_Lm, ("up", "low")[d])

        def rk_tensor(pe):
            pe.wait_ge(f["rk_w"], 80)
            pe.wait_ge(f["rk_tanh"], 1)
            for d in range(2):
                r = slice(64 * d, 64 * d + 64)
                for b in range(2):
                    cb = slice(b * P, (b + 1) * P)
                    pe.matmul(ps[:, 2 * d + b, 0:S], rk_w2[r, cb], U[r, U_WD, :], start=True, stop=True)
                    mm = pe.matmul(ps[:, 4 + 2 * d + b, 0:S], rk_a2[r, cb], U[r, U_AD, :], start=True, stop=True)
            mm.then_inc(f["rk_logits"], 1)
            pe.wait_ge(f["rk_kx"], 1)
            pe.wait_ge(f["rk_sig"], 1)
            for b in range(2):
                mm = pe.matmul(ps[:, b, 0:S], const("bdones"), rk_ev[:, b, :], start=True, stop=True)
            mm.then_inc(f["rk_kk2"], 1)
            pe.wait_ge(f["rk_vbd"], 1)
            for b in range(2):
                for c in range(NC):
                    mm = pe.matmul(ps[:, 2, (b * NC + c) * 64:(b * NC + c + 1) * 64], (bd_b, bd_k)[b][:, c, :],
                                   const("stack"), start=True, stop=True)
            mm.then_inc(f["rk_vps"], 1)
            for u, (d, b) in enumerate(UNITS):
                pe.wait_ge(f["rk_bd"], u + 1)
                for c in range(NC):
                    A, B, K = bd_ar[:, c, 0, :], bd_b[:, c, :], bd_k[:, c, :]
                    ar = bd_ar[:, c, :, :].rearrange("p k m -> p (k m)")
                    pe.matmul(ps[:, 0, c * P:(c + 1) * P], A, B, start=True, stop=True)
                    cc = (c % 2) * 2 * P
                    pe.matmul(ps[:, 1 + c // 2, cc:cc + 2 * P], B, ar, start=True, stop=True)
                    pe.matmul(ps[:, 3 + c // 2, cc:cc + 2 * P], K, ar, start=True, stop=True)
                    pe.transpose(ps[:, 5, c * P:(c + 1) * P], B, const("ident"))
                    mm = pe.transpose(ps[:, 6, c * P:(c + 1) * P], K, const("ident"))
                mm.then_inc(f["rk_toks"], 1)
                pe.wait_ge(f["rk_toks_sb"], u + 1)
                solve_tensor(pe, u, rk_Lm, rk_T, rk_TT, rk_Y)
                for k in range(NC):
                    c = k if d == 0 else NC - 1 - k
                    i = u * NC + k
                    pe.wait_ge(f["rk_S"], i + 1)
                    pe.matmul(ps[:, 6, 0:64], bd_ar[:, c, 0, :], rk_S, start=True, stop=False)
                    pe.matmul(ps[:, 6, 0:64], rk_MK[:, c, :], rk_V[:, b, c, :], start=False, stop=True) \
                      .then_inc(f["rk_rhs"], 1)
                    pe.wait_ge(f["rk_rhs_sb"], i + 1)
                    pe.matmul(ps[:, 7, 0:64], rk_TT[:, c, :], rk_rhs, start=True, stop=True).then_inc(f["rk_sa"], 1)
                    pe.wait_ge(f["rk_sa_sb"], i + 1)
                    pe.matmul(ps[:, 1, 0:64], const("ident"), rk_S, start=True, stop=False)
                    pe.matmul(ps[:, 1, 0:64], rk_Bt[:, c, :], rk_sa, start=False, stop=False)
                    pe.matmul(ps[:, 1, 0:64], rk_Kt[:, c, :], rk_V[:, b, c, :], start=False, stop=True)
                    pe.matmul(ps[:, 2, 0:64], bd_ar[:, c, 1, :], rk_S, start=True, stop=False)
                    pe.matmul(ps[:, 2, 0:64], rk_RB[:, c, :], rk_sa, start=False, stop=False)
                    pe.matmul(ps[:, 2, 0:64], rk_RK[:, c, :], rk_V[:, b, c, :], start=False, stop=True) \
                      .then_inc(f["rk_sy"], 1)
            pe.wait_ge(f["rk_prod"], 1)
            for b in range(2):
                pe.matmul(ps[:, b, 0:S], const("bdones"), rk_kd[:, b, :], start=True, stop=True)
                mm = pe.matmul(ps[:, 2 + b, 0:S], rk_g2[:, b * P:(b + 1) * P], U[:, U_GD, :], start=True, stop=True)
            mm.then_inc(f["rk_bonus"], 1)
            pe.wait_ge(f["rk_ybd"], 1)
            for b in range(2):
                for c in range(NC):
                    mm = pe.matmul(ps[:, 4 + b, c * 64:(c + 1) * 64], (bd_b, bd_k)[b][:, c, :], const("stack"),
                                   start=True, stop=True)
            mm.then_inc(f["rk_yT"], 1)

        def rk_vector(dve, l):
            d_ = dve.drain
            for z in (bd_ar.rearrange("p c k m -> p (c k m)"), bd_b, bd_k):
                dve.memset(z, 0.0)
            for b in range(2):
                ka = layer_vec("rwkv_k_a")(b)
                dve.tensor_scalar(rk_omka[:, b:b + 1], ka, -1.0, 1.0, ALU.mult, ALU.add)
                dve.tensor_scalar(rk_kk[:, b, :], U[:, U_K + b, :], layer_vec("rwkv_k_k")(b), None, ALU.mult)
            d_()
            dve.tensor_tensor(rk_ev, rk_kk, rk_kk, ALU.mult).then_inc(f["rk_kx"], 1)
            for b in range(2):
                for hh in range(2):
                    dve.tensor_copy(half((bd_b, bd_k)[b], hh), chunks(U[:, U_V + b, :], hh))
            d_().then_inc(f["rk_vbd"], 1)
            dve.wait_ge(f["rk_knorm"], 1)
            dve.tensor_scalar(rk_ei, rk_ei, 1e-12, None, ALU.max)
            d_()
            dve.reciprocal(rk_ei, rk_ei)
            d_()
            dve.tensor_tensor(rk_kk, rk_kk, rk_ei, ALU.mult)
            dve.wait_ge(f["rk_vps"], 1)
            dve.tensor_copy(rk_V, ps[:, 2, :].rearrange("p (b c v) -> p b c v", b=2, c=NC))
            d_()
            for d in range(2):
                sg, av = rk_sg[d], rk_a[d]
                for b in range(2):
                    dve.tensor_tensor_scan(rk_cum[:, b, :], const("reset"), sg[:, b, :], 0.0, ALU.mult, ALU.add)
                    dve.tensor_scalar(rk_kd[:, b, :], av[:, b, :], layer_vec("rwkv_k_a")(b), rk_omka[:, b:b + 1],
                                      ALU.mult, ALU.add)
                dve.tensor_tensor(rk_ab, rk_kk, av, ALU.mult)
                d_()
                c4 = rk_cum.rearrange("p b (c t) -> p b c t", c=NC)
                e4 = rk_exc.rearrange("p b (c t) -> p b c t", c=NC)
                dve.tensor_copy(rk_tot, c4[:, :, :, CH - 1])
                dve.tensor_tensor(rk_kd, rk_kd, U[:, U_K:U_K + 2, :], ALU.mult)
                if d == 0:
                    dve.tensor_tensor(rk_exc, rk_cum, sg, ALU.subtract)
                    d_().then_inc(f["rk_cums"], 1)
                    dve.tensor_copy(rk_ksum, rk_kd)
                else:
                    d_()
                    for b in range(2):
                        dve.tensor_tensor(e4[:, b], rk_tot[:, b, :].unsqueeze(2).to_broadcast([P, NC, CH]), c4[:, b],
                                          ALU.subtract)
                    d_()
                    dve.tensor_tensor(rk_cum, rk_exc, sg, ALU.add)
                    d_().then_inc(f["rk_cums"], 1)
                    dve.tensor_tensor(rk_ksum, rk_ksum, rk_kd, ALU.add)
                dve.wait_ge(f["rk_exps"], d + 1)
                for b in range(2):
                    u = 2 * d + b
                    for hh in range(2):
                        dve.scalar_tensor_tensor(out=half(bd_ar[:, :, 0, :], hh), in0=chunks(rk_kk[:, b, :], hh),
                                                 scalar=-1.0, in1=chunks(rk_ee[:, b, :], hh), op0=ALU.mult,
                                                 op1=ALU.mult)
                        dve.tensor_tensor(half(bd_ar[:, :, 1, :], hh), chunks(U[:, U_R + b, :], hh),
                                          chunks(rk_ei[:, b, :], hh), ALU.mult)
                        dve.tensor_tensor(half(bd_b, hh), chunks(rk_ab[:, b, :], hh), chunks(rk_ev[:, b, :], hh),
                                          ALU.mult)
                        dve.tensor_tensor(half(bd_k, hh), chunks(rk_kd[:, b, :], hh), chunks(rk_ev[:, b, :], hh),
                                          ALU.mult)
                    dve.memset(rk_S, 0.0)
                    d_().then_inc(f["rk_bd"], 1)
                    rk_unit_vector(dve, u, d, b)
            rk_finish_vector(dve)

        def rk_unit_vector(dve, u, d, b):
            d_ = dve.drain
            lo, up = ("low", "up") if d == 0 else ("up", "low")
            quads = [ps[:, 1 + 2 * k:3 + 2 * k, :].rearrange("p q (c k m) -> p (q c) k m", c=2, k=2) for k in range(2)]
            dve.wait_ge(f["rk_toks"], u + 1)
            dve.tensor_copy(rk_LT, quads[0][:, :, 0, :]).then_inc(f["sol_LT"], 1)
            solve_start_vector(dve, ps[:, 0, :].rearrange("p (c m) -> p c m", c=NC), rk_LT, rk_T, rk_TT, lo, up)
            dve.tensor_tensor(rk_MK, quads[1][:, :, 0, :], bc(const("strict_" + up), NC), ALU.mult)
            dve.tensor_tensor(rk_RK, quads[1][:, :, 1, :], bc(const("incl_" + up), NC), ALU.mult)
            dve.tensor_tensor(rk_RB, quads[0][:, :, 1, :], bc(const("incl_" + up), NC), ALU.mult)
            solve_vector(dve, u, rk_T, rk_TT, rk_Y)
            d_().then_inc(f["rk_S"], 1)
            for k in range(NC):
                c = k if d == 0 else NC - 1 - k
                i = u * NC + k
                dve.wait_ge(f["rk_rhs"], i + 1)
                dve.tensor_copy(rk_rhs, ps[:, 6, 0:64]).then_inc(f["rk_rhs_sb"], 1)
                dve.wait_ge(f["rk_sa"], i + 1)
                dve.tensor_copy(rk_sa, ps[:, 7, 0:64]).then_inc(f["rk_sa_sb"], 1)
                dve.wait_ge(f["rk_sy"], i + 1)
                st = dve.tensor_scalar(rk_S, ps[:, 1, 0:64], rk_tot[:, b, c:c + 1], None, ALU.mult)
                if k < NC - 1:
                    st.then_inc(f["rk_S"], 1)
                if d == 0:
                    dve.tensor_copy(rk_y[:, b, c, :], ps[:, 2, 0:64])
                else:
                    dve.tensor_tensor(rk_y[:, b, c, :], rk_y[:, b, c, :], ps[:, 2, 0:64], ALU.add)
            d_()

        def rk_finish_vector(dve):
            d_ = dve.drain
            dve.tensor_tensor(rk_kd, U[:, U_R:U_R + 2, :], rk_ksum, ALU.mult)
            yv = rk_y.rearrange("p b c v -> p (b c) v")
            sq = rk_T.rearrange("p c m -> p (c m)").rearrange("p (g v) -> p g v", v=64)
            dve.tensor_reduce(tiny[:, 40:48], yv, AX.X, ALU.add)
            d_()
            for b in range(2):
                dve.tensor_scalar(rk_kd[:, b, :], rk_kd[:, b, :], layer_vec("rwkv_r_k")(b), None, ALU.mult)
            dve.tensor_scalar(tiny[:, 40:48], tiny[:, 40:48], 1.0 / 64, None, ALU.mult)
            d_().then_inc(f["rk_prod"], 1)
            dve.tensor_tensor(yv, yv, tiny[:, 40:48].unsqueeze(2).to_broadcast([P, 8, 64]), ALU.subtract)
            d_()
            dve.tensor_tensor(sq, yv, yv, ALU.mult)
            d_()
            dve.tensor_reduce(tiny[:, 48:56], sq, AX.X, ALU.add).then_inc(f["rk_var"], 1)
            dve.wait_ge(f["rk_std"], 1)
            dve.reciprocal(tiny[:, 64:72], tiny[:, 56:64])
            d_()
            dve.tensor_tensor(yv, yv, tiny[:, 64:72].unsqueeze(2).to_broadcast([P, 8, 64]), ALU.mult)
            d_()
            for b in range(2):
                for hh in range(2):
                    r = slice(hh * 64, hh * 64 + 64)
                    dve.tensor_copy(half((bd_b, bd_k)[b], hh), rk_y[r, b, :, :])
            d_().then_inc(f["rk_ybd"], 1)
            dve.wait_ge(f["rk_bonus"], 1)
            dve.tensor_tensor(rk_ab, ps[:, 0:2, 0:S], U[:, U_V:U_V + 2, :], ALU.mult)
            dve.tensor_copy(rk_g, ps[:, 2:4, 0:S])
            dve.wait_ge(f["rk_yT"], 1)
            for b in range(2):
                dve.tensor_scalar(rk_ei[:, b, :], ps[:, 4 + b, 0:S], layer_vec("rwkv_lnx_g")(b),
                                  layer_vec("rwkv_lnx_b")(b), ALU.mult, ALU.add)
            d_()
            dve.tensor_tensor(rk_ei, rk_ei, rk_ab, ALU.add)
            d_()
            dve.tensor_tensor(rk_ei, rk_ei, rk_g, ALU.mult)
            d_()
            for b in range(2):
                put_y(dve, 2 + b, rk_ei[:, b, :])

        pool_a = work[:, 0:2048].rearrange("p (b t) -> p b t", b=C)
        pool_b = work[:, 2048:4096].rearrange("p (b t) -> p b t", b=C)
        pool_c = work[:, 4096:5120].rearrange("p (g t) -> p g t", g=4)
        pool_row = work[:, 5120:6144]
        pool_m = work[:, 6144:8192].rearrange("p (b t) -> p b t", b=C)

        def add_pool():
            tiles = D // GW

            def proj_stream(sp, n, l):
                project_stream(sp, n, w["pool_w_in_2"], 0, D)
                return n + tiles

            def proj_tensor(pe, n, l):
                norm_tensor(pe)
                project_tensor(pe, n, D)
                return n + tiles

            def proj_scalar(act, n, l):
                norm_scalar(act)
                norm_gain_scalar(act, second_vec("norm_mix_g_2"))
                project_scalar(act, n, D, U)
                return n + tiles

            def proj_vector(dve, n, l):
                norm_vector(dve, second_vec("norm_mix_g_2"))
                project_vector(dve, n, D, U)
                return n + tiles
            STREAM["pool_in"], TENSOR["pool_in"] = proj_stream, proj_tensor
            VECTOR["pool_in"], SCALAR["pool_in"] = proj_vector, proj_scalar

            def stream(sp, n, l):
                load_tile(sp, n, cols(a["pool_w_group_2"].rearrange("o g c e -> (o g c) e"), 0, 0))
                return n + 1

            def tensor(pe, n, l):
                open_y(pe, 2 * TT)
                pe.wait_ge(f["pooled"], 1)
                take_split(pe, n)
                for g in range(4):
                    for t in range(TT):
                        for b in range(2):
                            c = 2 * g + b
                            for k, (wp, part) in enumerate(PASSES):
                                mm = pe.matmul(ps[:, 2 * t + g // 2, (g % 2) * GW:(g % 2 + 1) * GW],
                                               (xhi, xlo)[part][:, c, t * P:(t + 1) * P],
                                               wp[:, n % SPLIT, c * GW:(c + 1) * GW], start=False,
                                               stop=(b == 1 and k == 2), skip_group_check=True)
                mm.then_inc(tile_done[n % SPLIT], 1)
                return n + 1

            def scalar(act, n, l):
                act.dma_start(pool_c, a["pool_counts"]).then_inc(f["decay_in"], 16)
                act.dma_start(pool_row, a["pool_scale_2"].rearrange("o d -> (o d)").partition_broadcast(P)) \
                   .then_inc(f["vecs"], 16)
                take(act, tile_done[n % SPLIT])
                split_hi(act, n + SPLIT)
                return n + 1

            def vector(dve, n, l):
                src = U
                for g in range(4):
                    s, lo = 2 ** g, 2 * g
                    dst = (pool_a, pool_b)[g % 2]
                    dve.tensor_tensor(dst[:, lo:C, s:S], src[:, lo:C, s:S], src[:, lo:C, 0:S - s], ALU.add)
                    dve.tensor_copy(dst[:, lo:C, 0:s], src[:, lo:C, 0:s])
                    dve.drain()
                    if g == 0:
                        dve.wait_ge(f["decay_in"], 16)
                    dve.tensor_tensor(pool_m[:, lo:lo + 2, :], dst[:, lo:lo + 2, :], bc(pool_c[:, g, :], 2), ALU.mult)
                    src = dst
                dve.drain()
                dve.tensor_tensor(pool_m, pool_m, U[:, 0:C, :], ALU.subtract)
                dve.drain()
                dve.tensor_copy(xhi[:, :, :], pool_m)
                dve.drain()
                dve.tensor_tensor(xlo[:, :, :], pool_m, xhi[:, :, :], ALU.subtract).then_inc(f["pooled"], 1)
                take(dve, hi_ready[n % SPLIT])
                split_lo(dve, n + SPLIT)
                dve.wait_ge(f["vecs"], 16)
                for t in range(TT):
                    y = (pool_a, pool_b)[t].rearrange("p b t -> p (b t)")[:, 0:D]
                    dve.tensor_tensor(y, ps[:, 2 * t:2 * t + 2, :].rearrange("p a b -> p (a b)"), pool_row, ALU.mult)
                dve.drain()
                for t in range(TT):
                    y = (pool_a, pool_b)[t].rearrange("p b t -> p (b t)")[:, 0:D]
                    dve.tensor_tensor(x[:, t, :], x[:, t, :], y, ALU.add)
                return n + 1
            STREAM["pool"], TENSOR["pool"], VECTOR["pool"], SCALAR["pool"] = stream, tensor, vector, scalar

        NH = 8
        DN_Q, DN_K, DN_V, DN_Z = 0, 8, 16, 24
        DN_W = 4 * NH * P

        def th(lo):
            return work[:, lo:lo + 2048].rearrange("p (t h m) -> p t h m", t=TT, h=NH)

        dn_v, dn_k, dn_TT, dn_qk = th(0), th(2048), th(4096), th(6144)
        dn_fm = work[:, 4096:8192].rearrange("p (b t) -> p b t", b=16)
        fresh_u = U.rearrange("p b t -> p (b t)")[:, DN_V * S:(DN_V + 8) * S]
        sol_T, sol_LT, sol_Y, sol_dec = (fresh_u[:, 512 * i:512 * i + 512].rearrange("p (c m) -> p c m", c=4)
                                         for i in range(4))
        sol_L = work[:, 8192:8704].rearrange("p (c m) -> p c m", c=4)
        sol_Lm = [work[:, 8704 + 512 * i:9216 + 512 * i].rearrange("p (c m) -> p c m", c=4) for i in range(2)]
        dn_S = fresh_u[:, 0:1024].rearrange("p (h m) -> p h m", h=NH)
        dn_rhs = fresh_u[:, 1024:2048].rearrange("p (h m) -> p h m", h=NH)
        dn_new = work[:, 8192:9216].rearrange("p (h m) -> p h m", h=NH)
        dn_upd = work[:, 9216:10240].rearrange("p (h m) -> p h m", h=NH)
        pt16 = lambda i: dn_tiny[:, 16 * i:16 * i + 16].rearrange("p (t h) -> p t h", t=TT)
        dn_beta, dn_g, dn_gc, dn_eg, dn_beg, dn_tail, dn_ms, dn_tmp, dn_ba, dn_ab2 = (pt16(i) for i in range(10))
        dn_last = dn_tiny[:, 160:192].rearrange("p (c h) -> p c h", c=NC)

        def dn_norm_small_scalar(act, src, cols_n):
            act.wait_ge(f["narrow_in"], 16)
            act.copy(nar_hi[:, 0:C * cols_n], nar[:, 0:C * cols_n]).then_inc(f["narrow_hi"], 1)

        def narrow_vector(dve, cols_n):
            dve.wait_ge(f["narrow_hi"], 1)
            dve.tensor_tensor(nar_lo[:, 0:C * cols_n], nar[:, 0:C * cols_n], nar_hi[:, 0:C * cols_n],
                              ALU.subtract).then_inc(f["narrow_lo"], 1)

        def narrow_tensor(pe, cols_n):
            pe.wait_ge(f["narrow_lo"], 1)
            for t in range(TT):
                for c in range(C):
                    for k, (wn, part) in enumerate(((nar_hi, 0), (nar_lo, 0), (nar_hi, 1))):
                        mm = pe.matmul(ps[:, 7, t * cols_n:(t + 1) * cols_n],
                                       (xhi, xlo)[part][:, c, t * P:(t + 1) * P],
                                       wn[:, c * cols_n:(c + 1) * cols_n], start=(c == 0 and k == 0),
                                       stop=(c == C - 1 and k == 2))
            mm.then_inc(f["narrow_done"], 1)

        def add_dn_in():
            tiles = DN_W // GW

            def stream(sp, n, l):
                project_stream(sp, n, w["dn_w_in_2"], 0, DN_W)
                return n + tiles

            def tensor(pe, n, l):
                norm_tensor(pe)
                pe.wait_ge(f["xt_ready"], C)
                narrow_tensor(pe, 16)
                project_tensor(pe, n, DN_W)
                return n + tiles

            def scalar(act, n, l):
                act.dma_start(nar[:, :].rearrange("p (c f) -> p c f", c=C), cols(w["dn_w_in_2"], 0, DN_W, 16)) \
                   .then_inc(f["narrow_in"], 16)
                act.dma_start(dn_rows[:, 0:8], a["dn_a_log_2"].rearrange("o h -> (o h)").partition_broadcast(P)) \
                   .then_inc(f["vecs"], 16)
                act.dma_start(dn_rows[:, 8:16], a["dn_dt_bias_2"].rearrange("o h -> (o h)").partition_broadcast(P)) \
                   .then_inc(f["vecs"], 16)
                norm_scalar(act)
                norm_gain_scalar(act, second_vec("norm_mix_g_2", C))
                dn_norm_small_scalar(act, None, 16)
                act.wait_ge(f["narrow_done"], 1)
                act.copy(dn_ba, ps[:, 7, 0:32].rearrange("p (t m) -> p t m", t=TT)[:, :, 0:8])
                act.copy(dn_ab2, ps[:, 7, 0:32].rearrange("p (t m) -> p t m", t=TT)[:, :, 8:16])
                act.wait_ge(f["vecs"], 32)
                project_scalar(act, n, DN_W, U)
                return n + tiles

            def vector(dve, n, l):
                norm_vector(dve, second_vec("norm_mix_g_2", C))
                narrow_vector(dve, 16)
                project_vector(dve, n, DN_W, U)
                return n + tiles
            STREAM["dn_in"], TENSOR["dn_in"], VECTOR["dn_in"], SCALAR["dn_in"] = stream, tensor, vector, scalar

        def bct(ap):
            return ap.unsqueeze(1).to_broadcast([P, TT, NH])

        QUADS = 6
        def dn_pre_scalar(act):
            act.activation(dn_beta, dn_ba, ACT.Sigmoid)
            act.wait_ge(f["dn_z"], 1)
            act.activation(dn_tmp, dn_ab2, ACT.Abs)
            act.drain()
            act.activation(dn_tmp, dn_tmp, ACT.Exp, scale=-1.0)
            act.drain()
            act.activation(dn_tmp, dn_tmp, ACT.Ln, bias=small("one"))
            act.activation(dn_rows[:, 0:8], dn_rows[:, 0:8], ACT.Exp).then_inc(f["dn_sp"], 1)
            act.wait_ge(f["dn_gc"], 1)
            act.activation(dn_eg, ps[:, 0, 0:16].rearrange("p (t h) -> p t h", t=TT), ACT.Exp)
            for odd in range(2):
                act.activation(dn_last.rearrange("p (k a) h -> p k a h", a=2)[:, :, odd, :],
                               ps[:, 2 + odd, 0:16].rearrange("p (k h) -> p k h", k=2), ACT.Exp)
            act.copy(dn_gc, ps[:, 0, 0:16].rearrange("p (t h) -> p t h", t=TT)).then_inc(f["dn_eg"], 1)
            act.wait_ge(f["dn_tail"], 1)
            act.activation(dn_tail, dn_tail, ACT.Exp)
            for i in range(QUADS):
                act.wait_ge(f["dn_conv"], i + 1)
                act.activation(U[:, 4 * i:4 * i + 4, :], dn_fm[:, 4 * (i % 2):4 * (i % 2) + 4, :],
                               ACT.Silu).then_inc(f["dn_silu"], 1)
            act.activation(U[:, DN_Z:DN_Z + 8, :], U[:, DN_Z:DN_Z + 8, :], ACT.Silu)
            for i in range(4):
                act.activation(dn_fm[:, 8 + 4 * (i % 2):12 + 4 * (i % 2), :], U[:, 4 * i:4 * i + 4, :], ACT.Square) \
                   .then_inc(f["dn_sq"], 1)
                act.wait_ge(f["dn_ss"], i + 1)
                if i >= 2:
                    act.wait_ge(f["dn_unit"], i - 1)
                act.activation(dn_fm[:, 0:4, :] if i % 2 == 0 else dn_fm[:, 4:8, :],
                               ps[:, 4 * (i % 2):4 * (i % 2) + 4, 0:S], ACT.Sqrt, bias=small("eps"),
                               ).then_inc(f["dn_rt"], 1)

        def dn_pre_vector(dve):
            d_ = dve.drain
            dve.tensor_tensor(dn_ab2, dn_ab2, bct(dn_rows[:, 8:16]), ALU.add).then_inc(f["dn_z"], 1)
            dve.wait_ge(f["dn_sp"], 1)
            dve.tensor_scalar(dn_g, dn_ab2, 0.0, None, ALU.max)
            d_()
            dve.tensor_tensor(dn_g, dn_g, dn_tmp, ALU.add)
            d_()
            dve.scalar_tensor_tensor(out=dn_g, in0=dn_g, scalar=-1.0, in1=bct(dn_rows[:, 0:8]), op0=ALU.mult,
                                     op1=ALU.mult).then_inc(f["dn_gr"], 1)
            dve.wait_ge(f["dn_eg"], 1)
            dve.tensor_tensor(dn_tail, ps[:, 1, 0:16].rearrange("p (t h) -> p t h", t=TT), dn_gc,
                              ALU.subtract).then_inc(f["dn_tail"], 1)
            dve.tensor_tensor(dn_beg, dn_beta, dn_eg, ALU.mult)
            for i in range(QUADS):
                if i >= 2:
                    dve.wait_ge(f["dn_silu"], i - 1)
                for j in range(4):
                    def step(k):
                        b = 4 * i + j
                        dst, s = dn_fm[:, 4 * (i % 2) + j, :], 3 - k
                        wk = second_vec("dn_conv_w_2")(24 * k + b)
                        if s == 0:
                            dve.tensor_scalar(dst, U[:, b, :], wk, None, ALU.mult)
                        else:
                            dve.scalar_tensor_tensor(out=dst[:, s:S], in0=U[:, b, 0:S - s], scalar=wk, in1=dst[:, s:S],
                                                     op0=ALU.mult, op1=ALU.add)
                    step(3)
                d_()
                for k in (2, 1, 0):
                    for j in range(4):
                        b = 4 * i + j
                        dst, s = dn_fm[:, 4 * (i % 2) + j, :], 3 - k
                        dve.scalar_tensor_tensor(out=dst[:, s:S], in0=U[:, b, 0:S - s],
                                                 scalar=second_vec("dn_conv_w_2")(24 * k + b), in1=dst[:, s:S],
                                                 op0=ALU.mult, op1=ALU.add)
                    st = d_()
                st.then_inc(f["dn_conv"], 1)
            for i in range(4):
                dve.wait_ge(f["dn_rt"], i + 1)
                rt = dn_fm[:, 4 * (i % 2):4 * (i % 2) + 4, :]
                dve.reciprocal(rt, rt)
                d_()
                u = U[:, 4 * i:4 * i + 4, :]
                if i < 2:
                    dve.scalar_tensor_tensor(out=u.rearrange("p b t -> p (b t)"), in0=u.rearrange("p b t -> p (b t)"),
                                             scalar=P ** -0.5, in1=rt.rearrange("p b t -> p (b t)"), op0=ALU.mult,
                                             op1=ALU.mult)
                else:
                    dve.tensor_tensor(u, u, rt, ALU.mult)
                d_().then_inc(f["dn_unit"], 1)

        def dn_pre_tensor(pe):
            pe.wait_ge(f["dn_gr"], 1)
            gf = dn_g.rearrange("p t h -> p (t h)")
            pe.matmul(ps[:, 0, 0:16], const("incl_up"), gf, start=True, stop=True)
            pe.matmul(ps[:, 1, 0:16], const("bdones"), gf, start=True, stop=True)
            for c in range(NC):
                r = slice((c % 2) * 64, (c % 2) * 64 + 64)
                mm = pe.matmul(ps[:, 2 + c % 2, (c // 2) * NH:(c // 2 + 1) * NH], const("ones")[r, :],
                               dn_g[r, c // 2, :], start=True, stop=True)
            mm.then_inc(f["dn_gc"], 1)
            for i in range(4):
                pe.wait_ge(f["dn_sq"], i + 1)
                if i == 0:
                    pe.wait_ge(f["dn_tail"], 1)
                for j in range(4):
                    mm = pe.matmul(ps[:, 4 * (i % 2) + j, 0:S], const("ones"), dn_fm[:, 8 + 4 * (i % 2) + j, :],
                                   start=True, stop=True)
                mm.then_inc(f["dn_ss"], 1)

        def dn_chunk_tensor(pe):
            for g in range(4):
                for j in range(4):
                    for t in range(TT):
                        h = 4 * (g % 2) + j
                        tr = pe.transpose(ps[:, 2 * (g % 2) + t, j * P:(j + 1) * P],
                                          U[:, (DN_V, DN_K)[g // 2] + h, t * P:(t + 1) * P], const("ident"))
                if g % 2 == 1:
                    tr.then_inc(f["dn_turned"], 1)
                    pe.wait_ge(f["dn_taken"], g // 2 + 1)
            for u in range(4):
                t, hs = u // 2, range(4 * (u % 2), 4 * (u % 2) + 4)
                pe.wait_ge(f["dn_diag"], u + 1)
                for j, h in enumerate(hs):
                    tk = slice(t * P, (t + 1) * P)
                    pe.matmul(ps[:, 1, j * P:(j + 1) * P], const("ones"), sol_Y[:, j, :], start=True, stop=True)
                    pe.matmul(ps[:, 2, j * P:(j + 1) * P], U[:, DN_K + h, tk], U[:, DN_K + h, tk], start=True, stop=True)
                    mm = pe.matmul(ps[:, 3, j * P:(j + 1) * P], U[:, DN_Q + h, tk], U[:, DN_K + h, tk], start=True,
                                   stop=True)
                mm.then_inc(f["dn_gram"], 1)
                pe.wait_ge(f["dn_L"], u + 1)
                for j in range(4):
                    pe.transpose(ps[:, 4, j * P:(j + 1) * P], sol_L[:, j, :], const("ident"))
                    tr = pe.transpose(ps[:, 6, j * P:(j + 1) * P], sol_T[:, j, :], const("ident"))
                tr.then_inc(f["dn_LT"], 1)
                solve_tensor(pe, u, sol_Lm, sol_T, dn_TTu(u), sol_Y)

        def dn_TTu(u):
            return dn_TT[:, u // 2, 4 * (u % 2):4 * (u % 2) + 4, :]

        def dn_chunk_scalar(act):
            for u in range(4):
                act.wait_ge(f["dn_dec"], u + 1)
                act.activation(sol_dec, sol_dec, ACT.Exp).then_inc(f["dn_exp"], 1)

        def dn_chunk_pool(pool):
            for u in range(4):
                solve_pool(pool, u, sol_LT, sol_Lm, "up")

        def dn_chunk_vector(dve):
            d_ = dve.drain
            for g in range(2):
                dve.wait_ge(f["dn_turned"], g + 1)
                for h in range(NH):
                    for t in range(TT):
                        src = ps[:, 2 * (h // 4) + t, (h % 4) * P:(h % 4 + 1) * P]
                        if g == 0:
                            dve.tensor_scalar(dn_v[:, t, h, :], src, dn_beta[:, t, h:h + 1], None, ALU.mult)
                        else:
                            dve.tensor_copy(dn_k[:, t, h, :], src)
                d_().then_inc(f["dn_taken"], 1)
            for u in range(4):
                t, hs = u // 2, slice(4 * (u % 2), 4 * (u % 2) + 4)
                gcs = dn_gc[:, t, hs].unsqueeze(2).to_broadcast([P, 4, P])
                dve.tensor_tensor(sol_Y, bc(const("ident"), 4), gcs, ALU.mult).then_inc(f["dn_diag"], 1)
                dve.wait_ge(f["dn_gram"], u + 1)
                dve.tensor_tensor(sol_dec, gcs, four(1), ALU.subtract)
                d_()
                dve.tensor_scalar(sol_dec, sol_dec, 0.0, None, ALU.min)
                d_().then_inc(f["dn_dec"], 1)
                dve.wait_ge(f["dn_exp"], u + 1)
                dve.tensor_tensor(sol_dec, sol_dec, bc(const("incl_low"), 4), ALU.mult)
                d_()
                dve.tensor_tensor(sol_L, four(2), sol_dec, ALU.mult)
                dve.tensor_tensor(sol_T, four(3), sol_dec, ALU.mult)
                d_()
                dve.scalar_tensor_tensor(out=sol_L, in0=sol_L, scalar=-1.0,
                                         in1=dn_beta[:, t, hs].unsqueeze(2).to_broadcast([P, 4, P]), op0=ALU.mult,
                                         op1=ALU.mult).then_inc(f["dn_L"], 1)
                dve.wait_ge(f["dn_LT"], u + 1)
                dve.tensor_copy(dn_qk[:, t, hs, :], four(6))
                dve.tensor_copy(sol_LT, four(4)).then_inc(f["sol_LT"], 1)
                d_()
                solve_start_vector(dve, sol_L, sol_LT, sol_T, dn_TTu(u), "low", "up")
                solve_vector(dve, u, sol_T, dn_TTu(u), sol_Y)
                d_()

        def two(bank):
            return ps[:, bank:bank + 2, :].rearrange("p a (h m) -> p (a h) m", h=4)

        def dn_scan_tensor(pe):
            for c in range(NC):
                t, tk = c // 2, slice((c // 2) * P, (c // 2 + 1) * P)
                r = slice((c % 2) * 64, (c % 2) * 64 + 64)
                pe.wait_ge(f["dn_S"], c + 1)
                for h in range(NH):
                    mm = pe.matmul(two(0)[:, h, :], U[:, DN_K + h, tk], dn_S[:, h, :], start=True, stop=True)
                mm.then_inc(f["dn_ks"], 1)
                for h in range(NH):
                    pe.matmul(two(2)[:, h, :], U[:, DN_Q + h, tk], dn_S[:, h, :], start=True, stop=True)
                pe.wait_ge(f["dn_rhs"], c + 1)
                for h in range(NH):
                    mm = pe.matmul(two(4)[:, h, :], dn_TT[:, t, h, :], dn_rhs[:, h, :], start=True, stop=True)
                mm.then_inc(f["dn_new"], 1)
                pe.wait_ge(f["dn_upd"], c + 1)
                for h in range(NH):
                    mm = pe.matmul(two(6)[:, h, :], dn_k[r, t, h, :], dn_upd[r, h, :], start=True, stop=True)
                mm.then_inc(f["dn_ku"], 1)
                for h in range(NH):
                    mm = pe.matmul(two(0)[:, h, :], dn_qk[:, t, h, :], dn_new[:, h, :], start=True, stop=True)
                mm.then_inc(f["dn_o"], 1)
            pe.wait_ge(f["dn_on"], 1)
            for h in range(NH):
                for t in range(TT):
                    tr = pe.transpose(ps[:, h, t * P:(t + 1) * P], dn_v[:, t, h, :], const("ident"))
                tr.then_inc(f["dn_oT"], 1)

        def dn_scan_scalar(act):
            act.wait_ge(f["dn_om"], 1)
            act.activation(dn_ms, dn_tmp, ACT.Sqrt, bias=small("eps"), scale=1.0 / P).then_inc(f["dn_or"], 1)

        def dn_scan_vector(dve):
            d_ = dve.drain

            def heads(ap, r=slice(0, P)):
                return ap[r].unsqueeze(2).to_broadcast([r.stop - r.start, NH, P])
            dve.memset(dn_S, 0.0)
            dve.memset(dn_new, 0.0)
            dve.memset(dn_upd, 0.0)
            d_().then_inc(f["dn_S"], 1)
            for c in range(NC):
                t = c // 2
                r = slice((c % 2) * 64, (c % 2) * 64 + 64)
                dve.wait_ge(f["dn_ks"], c + 1)
                dve.tensor_tensor(dn_rhs, two(0), heads(dn_beg[:, t, :]), ALU.mult)
                d_()
                dve.tensor_tensor(dn_rhs, dn_v[:, t, :, :], dn_rhs, ALU.subtract).then_inc(f["dn_rhs"], 1)
                dve.wait_ge(f["dn_new"], c + 1)
                dve.tensor_tensor(dn_upd, two(4), heads(dn_tail[:, t, :]), ALU.mult)
                dve.tensor_copy(dn_new, two(4))
                d_().then_inc(f["dn_upd"], 1)
                dve.tensor_tensor(dn_v[r, t, :, :], two(2)[r], heads(dn_eg[:, t, :], r), ALU.mult)
                dve.wait_ge(f["dn_ku"], c + 1)
                if c < NC - 1:
                    dve.tensor_tensor(dn_S, dn_S, heads(dn_last[:, c, :]), ALU.mult)
                    d_()
                    dve.tensor_tensor(dn_S, dn_S, two(6), ALU.add)
                d_()
                dve.wait_ge(f["dn_o"], c + 1)
                dve.tensor_tensor(dn_v[r, t, :, :], dn_v[r, t, :, :], two(0)[r], ALU.add)
                st = d_()
                if c < NC - 1:
                    st.then_inc(f["dn_S"], 1)
            sq = dn_k
            dve.tensor_tensor(sq, dn_v, dn_v, ALU.mult)
            d_()
            dve.tensor_reduce(dn_tmp, sq, AX.X, ALU.add).then_inc(f["dn_om"], 1)
            dve.wait_ge(f["dn_or"], 1)
            dve.reciprocal(dn_ms, dn_ms)
            d_()
            for t in range(TT):
                dve.tensor_tensor(dn_v[:, t, :, :], dn_v[:, t, :, :], heads(dn_ms[:, t, :]), ALU.mult)
            d_().then_inc(f["dn_on"], 1)
            out_t = dn_TT.rearrange("p t h m -> p (t h m)").rearrange("p (h t) -> p h t", h=NH)
            for h in range(NH):
                dve.wait_ge(f["dn_oT"], h + 1)
                dve.scalar_tensor_tensor(out=out_t[:, h, :], in0=ps[:, h, 0:S], scalar=second_vec("dn_norm_g_2")(0),
                                         in1=U[:, DN_Z + h, :], op0=ALU.mult, op1=ALU.mult)
            d_()
            dve.tensor_copy(xhi[:, :, :], out_t)
            d_()
            dve.tensor_tensor(xlo[:, :, :], out_t, xhi[:, :, :], ALU.subtract)

        TOP = 2
        OVER = 3
        ITEMS = E + OVER
        moe_x = xs
        moe_row = work[:, 3584:4608]
        ye = work[:, 4608:5632]
        m0 = 5632

        def mt(n, *dims):
            at = m_at[0]
            m_at[0] += n
            v = work[:, at:at + n]
            return v.rearrange("p (t e) -> p t e", t=TT) if dims else v
        m_at = [m0]
        pick = mt(2 * P, 1)
        gpick = mt(2 * P, 1)
        gpick_t = mt(2 * P)
        logit = mt(16, 1)
        gates = mt(16, 1)
        sel = mt(16, 1)
        hot1 = mt(16, 1)
        hot2 = mt(16, 1)
        tops = mt(16, 1)
        wts = mt(8, 1)
        slot_t = mt(2 * 16, 1)
        gate_t = mt(2 * 16, 1)
        idx_f = mt(16, 1)
        over = mt(8)
        pre = mt(8)
        hot_o = [mt(8) for _ in range(OVER)]
        mtmp = mt(8)
        bias_r = mt(8)
        ids_f = mt(16)

        def route_tensor(pe, n, l):
            norm_tensor(pe)
            pe.wait_ge(f["xt_ready"], C)
            narrow_tensor(pe, 8)
            pe.wait_ge(f["sel"], 1)
            pe.matmul(ps[:, 0, 0:8], const("tri"), sel[:, 0, :], start=True, stop=True)
            pe.matmul(ps[:, 0, 8:16], const("tri"), sel[:, 1, :], start=True, stop=False)
            pe.matmul(ps[:, 0, 8:16], const("ones"), sel[:, 0, :], start=False, stop=True)
            pe.matmul(ps[:, 1, 0:8], const("ones"), sel[:, 0, :], start=True, stop=False)
            pe.matmul(ps[:, 1, 0:8], const("ones"), sel[:, 1, :], start=False, stop=True).then_inc(f["ranks"], 1)
            return n

        def route_scalar(act, n, l):
            act.dma_start(nar[:, 0:C * E].rearrange("p (c f) -> p c f", c=C),
                          flat2(a["moe_router_w_2"]).rearrange("(c p) f -> p c f", p=P)).then_inc(f["narrow_in"], 16)
            act.dma_start(bias_r, a["moe_router_b_2"].rearrange("o e -> (o e)").partition_broadcast(P)) \
               .then_inc(f["vecs"], 16)
            act.dma_start(moe_row, a["norm_ffn_g_2"][1, :].partition_broadcast(P)).then_inc(f["vecs"], 16)
            norm_scalar(act)
            norm_gain_scalar(act, second_vec("norm_ffn_g_2", C))
            dn_norm_small_scalar(act, None, E)
            act.wait_ge(f["top"], 1)
            act.activation(wts[:, :, 0:1], wts[:, :, 1:2], ACT.Exp).then_inc(f["top_exp"], 1)
            return n

        def route_vector(dve, n, l):
            d_ = dve.drain
            norm_vector(dve, second_vec("norm_ffn_g_2", C))
            narrow_vector(dve, E)
            dve.wait_ge(f["vecs"], 32)
            for t in range(TT):
                dve.tensor_tensor(moe_x[:, t, :], moe_x[:, t, :], moe_row, ALU.mult)
            dve.wait_ge(f["narrow_done"], 1)
            dve.tensor_tensor(logit, ps[:, 7, 0:16].rearrange("p (t e) -> p t e", t=TT),
                              bias_r.unsqueeze(1).to_broadcast([P, TT, E]), ALU.add)
            d_()
            for t in range(TT):
                dve.max(tops[:, t, :], logit[:, t, :])
            d_()
            for t in range(TT):
                dve.max_index(idx_u[:, t, :], tops[:, t, :], logit[:, t, :])
            dve.tensor_tensor(wts[:, :, 1:2], tops[:, :, 1:2], tops[:, :, 0:1], ALU.subtract)
            d_().then_inc(f["top"], 1)
            dve.tensor_copy(idx_f, idx_u[:, :, :])
            dve.wait_ge(f["top_exp"], 1)
            dve.tensor_scalar(wts[:, :, 2:3], wts[:, :, 0:1], 1.0, None, ALU.add)
            d_()
            dve.reciprocal(wts[:, :, 3:4], wts[:, :, 2:3])
            d_()
            dve.tensor_tensor(wts[:, :, 2:3], wts[:, :, 3:4], wts[:, :, 0:1], ALU.mult)
            d_()
            for t in range(TT):
                io = const("iota", 0, E)
                dve.tensor_scalar(hot1[:, t, :], io, idx_f[:, t, 0:1], None, ALU.is_equal)
                dve.tensor_scalar(hot2[:, t, :], io, idx_f[:, t, 1:2], None, ALU.is_equal)
            d_()
            dve.tensor_tensor(sel, hot1, hot2, ALU.add).then_inc(f["sel"], 1)
            for t in range(TT):
                dve.tensor_scalar(gates[:, t, :], hot1[:, t, :], wts[:, t, 3:4], None, ALU.mult)
            d_()
            for t in range(TT):
                dve.scalar_tensor_tensor(out=gates[:, t, :], in0=hot2[:, t, :], scalar=wts[:, t, 2:3],
                                         in1=gates[:, t, :], op0=ALU.mult, op1=ALU.add)
            dve.wait_ge(f["ranks"], 1)
            dve.scalar_tensor_tensor(out=hot1, in0=ps[:, 0, 0:16].rearrange("p (t e) -> p t e", t=TT), scalar=1.0,
                                     in1=sel, op0=ALU.add, op1=ALU.mult)
            dve.tensor_scalar(over, ps[:, 1, 0:8], float(P), None, ALU.is_gt)
            d_()
            dve.tensor_tensor_scan(pre, const("ones", 0, 8), over, 0.0, ALU.mult, ALU.add)
            dve.tensor_scalar(slot_t[:, :, 0:E], hot1, -1.0, None, ALU.add)
            dve.tensor_copy(gate_t[:, :, 0:E], gates)
            dve.memset(ids_f, 0.0)
            d_()
            dve.tensor_copy(ids_f[:, 0:E], const("iota", 0, E))
            for k in range(OVER):
                dve.tensor_scalar(hot_o[k], pre, float(k + 1), None, ALU.is_equal)
            dve.tensor_scalar(ids_f[:, 12:13], pre[:, 7:8], float(E), None, ALU.add)
            d_()
            for k in range(OVER):
                dve.tensor_tensor(hot_o[k], hot_o[k], over, ALU.mult)
                d_()
                for dst, src in ([(slot_t[:, t, E + k:E + k + 1], hot1[:, t, :]) for t in range(TT)]
                                 + [(gate_t[:, t, E + k:E + k + 1], gates[:, t, :]) for t in range(TT)]
                                 + [(ids_f[:, E + k:E + k + 1], const("iota", 0, E))]):
                    dve.tensor_tensor(mtmp, src, hot_o[k], ALU.mult)
                    d_()
                    dve.tensor_reduce(dst, mtmp, AX.X, ALU.add)
                    d_()
            dve.tensor_scalar(slot_t[:, :, E:ITEMS], slot_t[:, :, E:ITEMS], -1.0 - P, None, ALU.add)
            dve.tensor_copy(ids[0:1, :], ids_f[0:1, :])
            d_().then_inc(items_ready, 1)
            return n

        def moe_stream(sp, n, l):
            wg, wu, wd = (a[k].rearrange("o e r c -> (o e r) c") for k in ("moe_w_gate_2", "moe_w_up_2",
                                                                          "moe_w_down_2"))

            def expert(i):
                return sp.value_load(ids[0:1, bass.ds(i, 1)], min_val=0, max_val=E - 1)

            def gate(m, e, g):
                load_tile(sp, m, cols(wg, e * D, g * GW))

            def up(m, e, g):
                load_tile(sp, m, cols(wu, e * D, g * GW))

            def down_(m, e, g):
                load_tile(sp, m, cols(wd, e * EF + g * GW, 0, D, 2))
            gate(n, 0, 0)
            up(n + 1, 0, 0)
            gate(n + 2, 0, 1)
            take(sp, items_ready)
            count = sp.value_load(ids[0:1, 12:13], min_val=E, max_val=ITEMS)
            with sp.Fori(0, count) as i:
                e = expert(i)
                up(n + 3, e, 1)
                m = n + 4
                with sp.Fori(0, (EG - 2) // 2) as j:
                    for k in range(2):
                        g = j * 2 + (2 + k)
                        gate(m + 3 * k, e, g)
                        up(m + 3 * k + 1, e, g)
                        down_(m + 3 * k + 2, e, j * 2 + k)
                m += 3 * (EG - 2)
                down_(m, e, EG - 2)
                down_(m + 1, e, EG - 1)
                nxt = expert(i + 1)
                gate(m + 2, nxt, 0)
                up(m + 3, nxt, 0)
                gate(m + 4, nxt, 1)
            return n

        def expert_tensor(pe, n):
            def by_token(m, dst):
                take_split(pe, m)
                for c in range(C):
                    for k, (w, part) in enumerate(PASSES):
                        mm = pe.matmul(dst, (xhi, xlo)[part][:, c, 0:P], w[:, m % SPLIT, c * GW:(c + 1) * GW],
                                       start=(c == 0 and k == 0), stop=(c == C - 1 and k == 2))
                mm.then_inc(tile_done[m % SPLIT], 1)

            def gate_up(m, q):
                by_token(m, ps[:, 4 + q, 0:GW])
                by_token(m + 1, ps[:, 6 + q, 0:GW])

            def turn(q):
                take(pe, hid_made[q])
                for b in range(2):
                    tr = pe.transpose(ps[:, 2 + q, b * P:(b + 1) * P], hid[:, q * GW + b * P:q * GW + (b + 1) * P],
                                      const("ident"))
                tr.then_inc(hid_turned[q], 1)

            def step(m, q):
                gate_up(m, q)
                turn(1 - q)
                take(pe, hid_ready[q])
                down(pe, m + 2, hidden(q), 1, False)

            pe.wait_ge(f["xt_ready"], C)
            open_y(pe, 2)
            gate_up(n, 0)
            gate_up(n + 2, 1)
            turn(0)
            with pe.Fori(0, (EG - 2) // 2):
                step(n + 4, 0)
                step(n + 7, 1)
            m = n + 3 * EG - 2
            take(pe, hid_ready[0])
            down(pe, m, hidden(0), 1, False)
            turn(1)
            take(pe, hid_ready[1])
            down(pe, m + 1, hidden(1), 1, True)

        def expert_scalar(act, n):
            def gate_up(m, q):
                take(act, tile_done[m % SPLIT])
                act.activation(sil[:, q, 0:GW], ps[:, 4 + q, 0:GW], ACT.Silu)
                split_hi(act, m + SPLIT)
                take(act, tile_done[(m + 1) % SPLIT])
                split_hi(act, m + 1 + SPLIT)

            def turned(q):
                take(act, hid_turned[q])
                act.copy(hhi[:, q, :, 0:P], ps[:, 2 + q, 0:GW].rearrange("p (b t) -> p b t", b=2)) \
                   .then_inc(hid_hi[q], 1)

            def next_split(m):
                take(act, tile_done[m % SPLIT])
                split_hi(act, m + SPLIT)

            def step(m, q):
                gate_up(m, q)
                turned(1 - q)
                next_split(m + 2)

            gate_up(n, 0)
            gate_up(n + 2, 1)
            turned(0)
            with act.Fori(0, (EG - 2) // 2):
                step(n + 4, 0)
                step(n + 7, 1)
            m = n + 3 * EG - 2
            next_split(m)
            turned(1)
            next_split(m + 1)

        def expert_vector(dve, n):
            def refill(m):
                take(dve, hi_ready[m % SPLIT])
                split_lo(dve, m)

            def gate_up(m, q):
                refill(m + SPLIT)
                refill(m + 1 + SPLIT)
                dve.tensor_tensor(hid[:, q * GW:(q + 1) * GW], ps[:, 6 + q, 0:GW], sil[:, q, 0:GW],
                                  ALU.mult).then_inc(hid_made[q], 1)

            def turned(q):
                take(dve, hid_hi[q])
                dve.tensor_tensor(hlo[:, q, :, 0:P], ps[:, 2 + q, 0:GW].rearrange("p (b t) -> p b t", b=2),
                                  hhi[:, q, :, 0:P], ALU.subtract).then_inc(hid_ready[q], 1)

            def step(m, q):
                gate_up(m, q)
                turned(1 - q)
                refill(m + 2 + SPLIT)

            gate_up(n, 0)
            gate_up(n + 2, 1)
            turned(0)
            with dve.Fori(0, (EG - 2) // 2):
                step(n + 4, 0)
                step(n + 7, 1)
            m = n + 3 * EG - 2
            refill(m + SPLIT)
            turned(1)
            refill(m + 1 + SPLIT)

        def items(eng, name, body):
            count = eng.value_load(ids[0:1, 12:13], min_val=E, max_val=ITEMS)
            with eng.Fori(0, count) as i:
                body(i)
                if name is None:
                    section_end_pool(eng)
                else:
                    section_end(eng, name)

        def moe_tensor(pe, n, l):
            def body(i):
                pe.wait_ge(f["picked"], 1)
                for t in range(TT):
                    tr = pe.transpose(ps[:, 7, t * P:(t + 1) * P], gpick[:, t, :], const("ident"))
                for c in range(C):
                    for t in range(TT):
                        mm = pe.matmul(ps[:, 2 + c // 4, (c % 4) * P:(c % 4 + 1) * P], moe_x[:, t, c * P:(c + 1) * P],
                                       pick[:, t, :], start=(t == 0), stop=(t == TT - 1))
                    if c % 4 == 3:
                        mm.then_inc(f["gathered"], 1)
                expert_tensor(pe, n)
                pe.wait_ge(f["ye"], 1)
                for t in range(TT):
                    for s in range(2):
                        mm = pe.matmul(ps[:, 2 + 2 * t + s, :], gpick_t[:, t * P:(t + 1) * P], ye[:, s * HALF:(s + 1) * HALF],
                                       start=True, stop=True)
                        mm.then_inc(f["back"], 1)
            items(pe, "pe", body)
            return n

        def moe_scalar(act, n, l):
            def body(i):
                for b in range(2):
                    act.wait_ge(f["gathered"], b + 1)
                    act.copy(xhi[:, 4 * b:4 * b + 4, 0:P], four(2 + b)).then_inc(f["norm_hi"], 1)
                act.copy(gpick_t, ps[:, 7, 0:2 * P]).then_inc(f["gt"], 1)
                expert_scalar(act, n)
            items(act, "act", body)
            return n

        def moe_vector(dve, n, l):
            def body(i):
                io = const("iota")
                for t in range(TT):
                    s = slot_t[:, t, bass.ds(i, 1)]
                    dve.tensor_scalar(pick[:, t, :], io, s, None, ALU.is_equal)
                    dve.tensor_scalar(gpick[:, t, :], io, s, gate_t[:, t, bass.ds(i, 1)], ALU.is_equal, ALU.mult)
                dve.drain().then_inc(f["picked"], 1)
                for b in range(2):
                    dve.wait_ge(f["norm_hi"], b + 1)
                    dve.tensor_tensor(xlo[:, 4 * b:4 * b + 4, 0:P], four(2 + b), xhi[:, 4 * b:4 * b + 4, 0:P],
                                      ALU.subtract).then_inc(f["xt_ready"], C // 2)
                dve.wait_ge(f["gt"], 1)
                expert_vector(dve, n)
                dve.tensor_copy(ye, ps[:, 0:2, :].rearrange("p a b -> p (a b)")).then_inc(f["ye"], 1)
                for t in range(TT):
                    for s in range(2):
                        dve.wait_ge(f["back"], 2 * t + s + 1)
                        xv = x[:, t, s * HALF:(s + 1) * HALF]
                        dve.tensor_tensor(xv, xv, ps[:, 2 + 2 * t + s, :], ALU.add)
            items(dve, "dve", body)
            return n

        def moe_pool(pool, n, l):
            items(pool, None, lambda i: None)

        def flat2(w):
            return w.rearrange("l r c -> (l r) c")

        w = {k: flat2(a[k]) for k in ("ffn1_w_gate", "ffn1_w_up", "ffn1_w_down", "ffn2_w_gate", "ffn2_w_up",
                                      "ffn2_w_down", "w_in", "w_out", "ffn_w_gate_2", "ffn_w_up_2",
                                      "ffn_w_down_2", "pool_w_in_2", "dn_w_in_2", "dn_w_out_2")}
        STREAM, TENSOR, VECTOR, SCALAR, POOL = {}, {}, {}, {}, {}

        def add_ffn(part, gain, names, scale, in_layers):
            def stream(sp, n, l):
                row = l * D if in_layers else 0
                frow = l * FF if in_layers else 0
                ffn_stream(sp, n, *(w[k] for k in names), row, frow, FG)
                return n + 3 * FG

            def tensor(pe, n, l):
                norm_tensor(pe)
                ffn_tensor(pe, n, FG)
                return n + 3 * FG

            def vector(dve, n, l):
                norm_vector(dve, gain)
                ffn_vector(dve, n, FG)
                add_y(dve, scale)
                return n + 3 * FG

            def scalar(act, n, l):
                norm_scalar(act)
                norm_gain_scalar(act, gain)
                ffn_scalar(act, n, FG)
                return n + 3 * FG
            STREAM[part], TENSOR[part], VECTOR[part], SCALAR[part] = stream, tensor, vector, scalar

        add_ffn("ffn1", layer_vec("ffn1_norm"), ("ffn1_w_gate", "ffn1_w_up", "ffn1_w_down"), 0.5, True)
        add_ffn("ffn2", layer_vec("ffn2_norm"), ("ffn2_w_gate", "ffn2_w_up", "ffn2_w_down"), 0.5, True)
        add_ffn("ffn3", second_vec("norm_ffn_g_2"), ("ffn_w_gate_2", "ffn_w_up_2", "ffn_w_down_2"), 1.0, False)

        same = lambda eng, n, l: n

        def pick_vectors(dve, n, l):
            dve.tensor_copy(cur[:, :], vec[:, bass.ds(l * NLV, NLV)])
            return n
        STREAM["vectors"], TENSOR["vectors"], VECTOR["vectors"], SCALAR["vectors"] = same, same, pick_vectors, same

        def add_final(part, gain):
            grow = work[:, 1536 + TT * D:1536 + (TT + 1) * D]

            def scalar(act, n, l):
                act.dma_start(grow, a[gain].partition_broadcast(P)).then_inc(f["vecs"], 16)
                norm_scalar(act)
                return n

            def vector(dve, n, l):
                dve.wait_ge(f["norm_root"], 1)
                dve.reciprocal(tiny[:, 4:6], tiny[:, 2:4])
                dve.drain()
                dve.wait_ge(f["vecs"], 16)
                for t in range(TT):
                    dve.scalar_tensor_tensor(out=x[:, t, :], in0=x[:, t, :], scalar=tiny[:, 4 + t:5 + t],
                                             in1=grow, op0=ALU.mult, op1=ALU.mult)
                return n
            STREAM[part], TENSOR[part], VECTOR[part], SCALAR[part] = same, same, vector, scalar

        add_final("final1", "final_norm")
        add_final("final2", "final_norm_g_2")
        add_project()
        add_out("out", "w_out")

        def add_mix(part, tensor, vector, scalar, pool=None):
            def wrap(fn):
                def go_on(eng, n, l):
                    if fn is not None:
                        fn(eng, l) if fn.__code__.co_argcount == 2 else fn(eng)
                    return n
                return go_on
            STREAM[part] = lambda sp, n, l: n
            TENSOR[part], VECTOR[part], SCALAR[part], POOL[part] = wrap(tensor), wrap(vector), wrap(scalar), wrap(pool)

        add_mix("ret", ret_tensor, ret_vector, ret_scalar)
        add_mix("mla", mla_tensor, mla_vector, mla_scalar)
        add_mix("rwkv", rk_tensor, rk_vector, rk_scalar, rk_pool)
        add_pool()
        add_dn_in()
        add_mix("dn_pre", dn_pre_tensor, dn_pre_vector, dn_pre_scalar)
        add_mix("dn_chunk", dn_chunk_tensor, dn_chunk_vector, dn_chunk_scalar, dn_chunk_pool)
        add_mix("dn_scan", dn_scan_tensor, dn_scan_vector, dn_scan_scalar)
        add_out("dn_out", "dn_w_out_2", lambda l: 0)
        STREAM["route"] = lambda sp, n, l: n
        TENSOR["route"], VECTOR["route"], SCALAR["route"] = route_tensor, route_vector, route_scalar
        STREAM["moe"], TENSOR["moe"], VECTOR["moe"], SCALAR["moe"] = moe_stream, moe_tensor, moe_vector, moe_scalar
        POOL["moe"] = moe_pool
        block = ctx.enter_context(nc.Block())

        @block.sync
        def _(sp):
            start_sync(sp)
            with sp.Fori(0, DEPTH) as l:
                n = 0
                for part in LAYER_PLAN:
                    n = STREAM[part](sp, n, l)
            assert n % RAW == 0
            for part in SECOND_PLAN:
                n = STREAM[part](sp, n, None)
            sp.wait_ge(f["x_out"], 1)
            sp.dma_start(out.rearrange("o (t p) d -> p (o t) d", p=P), x[:, :, :]).then_inc(f["x_in"], 16)
            sp.wait_ge(f["x_in"], 16)

        def run(eng, name, table, start):
            start(eng)
            section_end(eng, name)
            with eng.Fori(0, DEPTH) as l:
                n = 0
                for part in LAYER_PLAN:
                    n = table[part](eng, n, l)
                    section_end(eng, name)
            for part in SECOND_PLAN:
                n = table[part](eng, n, None)
                section_end(eng, name)

        @block.tensor
        def _(pe):
            run(pe, "pe", TENSOR, start_tensor)

        @block.vector
        def _(dve):
            run(dve, "dve", VECTOR, start_vector)
            dve.drain().then_inc(f["x_out"], 1)

        @block.scalar
        def _(act):
            run(act, "act", SCALAR, start_scalar)

        @block.gpsimd
        def _(pool):
            section_end_pool(pool)
            with pool.Fori(0, DEPTH) as l:
                for part in LAYER_PLAN:
                    POOL.get(part, lambda *a: None)(pool, 0, l)
                    section_end_pool(pool)
            for part in SECOND_PLAN:
                POOL.get(part, lambda *a: None)(pool, 0, None)
                section_end_pool(pool)


INPUTS = ["x", "positions", "ffn1_norm", "ffn1_w_gate", "ffn1_w_up", "ffn1_w_down", "mix_norm", "w_in", "w_out",
          "conv_w", "rwkv_w0_f", "rwkv_w0_b", "rwkv_w2_f", "rwkv_w2_b", "rwkv_a0_f", "rwkv_a0_b", "rwkv_a2_f",
          "rwkv_a2_b", "rwkv_g2", "rwkv_k_k", "rwkv_k_a", "rwkv_r_k", "rwkv_lnx_g", "rwkv_lnx_b", "ret_gn_g",
          "mla_q_a_norm", "mla_q_b", "mla_kv_a_norm", "mla_kv_b", "ffn2_norm", "ffn2_w_gate", "ffn2_w_up",
          "ffn2_w_down", "final_norm", "norm_mix_g_2", "norm_ffn_g_2", "pool_w_in_2", "pool_w_group_2",
          "pool_scale_2", "dn_w_in_2", "dn_conv_w_2", "dn_a_log_2", "dn_dt_bias_2", "dn_norm_g_2", "dn_w_out_2",
          "ffn_w_gate_2", "ffn_w_up_2", "ffn_w_down_2", "moe_router_w_2", "moe_router_b_2", "moe_w_gate_2",
          "moe_w_up_2", "moe_w_down_2", "final_norm_g_2"]


def kernel(**inputs):
    import concourse.bacc as _bacc
    from concourse.bass_utils import run_bass_kernel_spmd as _run

    nc = _bacc.Bacc("TRN2", target_bir_lowering=False, num_devices=1, dynamic_dma_scratch_size=1024)
    arrays, aps = {}, {}
    for name in INPUTS:
        v = np.ascontiguousarray(inputs[name])
        arrays[f"in_{name}"] = v
        aps[name] = nc.dram_tensor(f"in_{name}", v.shape, mybir.dt.from_np(v.dtype), kind="ExternalInput").ap()
    for name, v in (("consts", constants()), ("decay", retention_decay()), ("pool_counts", pool_counts())):
        arrays[f"const_{name}"] = v
        aps[name] = nc.dram_tensor(f"const_{name}", v.shape, F32, kind="ExternalInput").ap()
    y = nc.dram_tensor("out_0", (1, S, D), F32, kind="ExternalOutput").ap()
    build(nc, aps, y)
    r = _run(nc, [arrays], core_ids=[0])
    return r.results[0]["out_0"]
```
